# Optimizing a Trainium2 kernel written in Bass

```python
import jax, jax.numpy as jnp
from jax import lax
import numpy as np

D_MODEL = 1024
BATCH = 1
SEQ = 128
DEPTH = 2
DEC_BATCH = 1
DEC_SEQ = 512
PAST_LEN = 128

GRID_W = 64
ROPE_THETA = 10000.0
Q_BLOCK = 128
EPS = 1e-6
HEAD_DIM = 64
CHUNK = 128
A_GROUPS = 8
A_GROUP_DIM = 64
A_WIDTH = A_GROUPS * A_GROUP_DIM
B_HEADS = 8
B_KV_HEADS = 2
B_GROUP = B_HEADS // B_KV_HEADS
B_WIDTH = B_HEADS * HEAD_DIM
EV_IN = 2 * A_WIDTH + B_WIDTH + 2 * B_KV_HEADS * HEAD_DIM
EV_SPLITS = (A_WIDTH, 2 * A_WIDTH, 2 * A_WIDTH + B_WIDTH, 2 * A_WIDTH + B_WIDTH + B_KV_HEADS * HEAD_DIM)
EV_OUT = A_WIDTH + B_WIDTH
C_HEADS = 8
C_NOPE = 64
C_ROPE = 32
C_V = 64
C_Q_LORA = 256
C_KV_LORA = 128
C_WIDTH = C_HEADS * C_V
D_WIDTH = 512
D_CONV = 3
OD_IN = C_Q_LORA + C_KV_LORA + C_ROPE + 3 * D_WIDTH
OD_SPLITS = (C_Q_LORA, C_Q_LORA + C_KV_LORA, C_Q_LORA + C_KV_LORA + C_ROPE,
             C_Q_LORA + C_KV_LORA + C_ROPE + D_WIDTH, C_Q_LORA + C_KV_LORA + C_ROPE + 2 * D_WIDTH)
OD_OUT = C_WIDTH + D_WIDTH
N_EXPERTS = 16
EXPERT_FF = 512
EC_CAPACITY = 2
N_EVEN = (DEPTH + 1) // 2
N_ODD = DEPTH // 2

kernel_name = 'hybrid_diffusion_prefix_trunk_step'

def rms_norm(x, g):
    xf = x.astype(jnp.float32)
    y = xf * lax.rsqrt(jnp.mean(xf * xf, axis=-1, keepdims=True) + EPS)
    return (y * g.astype(jnp.float32)).astype(x.dtype)

def grid_angles(n_tokens, rot_dim):
    n_rows = n_tokens // GRID_W
    rows = jnp.repeat(jnp.arange(n_rows, dtype=jnp.float32), GRID_W)
    cols = jnp.tile(jnp.arange(GRID_W, dtype=jnp.float32), n_rows)
    axis_dim = rot_dim // 2
    inv_freq = ROPE_THETA ** (-jnp.arange(0, axis_dim, 2, dtype=jnp.float32) / axis_dim)
    return rows[:, None] * inv_freq, cols[:, None] * inv_freq

def rope_1d(x, ang):
    x1, x2 = jnp.split(x, 2, axis=-1)
    cos = jnp.cos(ang).astype(x.dtype)
    sin = jnp.sin(ang).astype(x.dtype)
    return jnp.concatenate([x1 * cos - x2 * sin, x2 * cos + x1 * sin], axis=-1)

def axial_rope(x, ang_row, ang_col):
    xr, xc = jnp.split(x, 2, axis=-1)
    return jnp.concatenate([rope_1d(xr, ang_row), rope_1d(xc, ang_col)], axis=-1)

def block_attention(q, k, v):
    b, hk, g, t, d = q.shape
    nb = t // Q_BLOCK
    qb = jnp.moveaxis(q.reshape(b, hk, g, nb, Q_BLOCK, d), 3, 0)
    scale = d ** -0.5

    def one_block(qi):
        s = jnp.einsum('bkgqd,bksd->bkgqs', qi, k, preferred_element_type=jnp.float32) * scale
        p = jax.nn.softmax(s, axis=-1).astype(v.dtype)
        return jnp.einsum('bkgqs,bksd->bkgqd', p, v)

    o = lax.map(one_block, qb)
    return jnp.moveaxis(o, 0, 3).reshape(b, hk, g, t, v.shape[-1])

def merge_heads(o):
    b, hk, g, t, d = o.shape
    return o.transpose(0, 3, 1, 2, 4).reshape(b, t, hk * g * d)

def modulation(cvec, w_mod, b_mod):
    m = jax.nn.silu(cvec) @ w_mod + b_mod
    return [p[:, None, :] for p in jnp.split(m, 6, axis=-1)]

def chunk_gating(u, va, w_s, b_s):
    b, t, _ = u.shape
    vc = va.reshape(b, t // CHUNK, CHUNK, A_GROUPS, A_GROUP_DIM)
    s = jnp.einsum('gpq,bnqgc->bnpgc', w_s, vc) + b_s.T[None, None, :, :, None]
    return u * s.reshape(b, t, A_WIDTH)

def even_project(h, w_in, q_gain, k_gain):
    b, t, _ = h.shape
    u, va, q, k, v = jnp.split(h @ w_in, list(EV_SPLITS), axis=-1)
    q = rms_norm(q.reshape(b, t, B_KV_HEADS, B_GROUP, HEAD_DIM), q_gain).transpose(0, 2, 3, 1, 4)
    k = rms_norm(k.reshape(b, t, B_KV_HEADS, HEAD_DIM), k_gain).transpose(0, 2, 1, 3)
    v = v.reshape(b, t, B_KV_HEADS, HEAD_DIM).transpose(0, 2, 1, 3)
    return u, va, q, k, v

def even_context(h, w_in, q_gain, k_gain, w_s, b_s, w_out):
    u, va, q, k, v = even_project(h, w_in, q_gain, k_gain)
    o = block_attention(q, k, v)
    out = jnp.concatenate([chunk_gating(u, va, w_s, b_s), merge_heads(o)], axis=-1) @ w_out
    return out, k, v

def even_latent(h, k_ctx, v_ctx, w_in, q_gain, k_gain, w_s, b_s, w_out):
    t = h.shape[1]
    u, va, q, k, v = even_project(h, w_in, q_gain, k_gain)
    ang_r, ang_c = grid_angles(t, HEAD_DIM)
    q = axial_rope(q, ang_r, ang_c)
    k = axial_rope(k, ang_r, ang_c)
    o = block_attention(q, jnp.concatenate([k_ctx, k], axis=2), jnp.concatenate([v_ctx, v], axis=2))
    return jnp.concatenate([chunk_gating(u, va, w_s, b_s), merge_heads(o)], axis=-1) @ w_out

def odd_project(h, w_in, q_a_norm, kv_a_norm, w_uq):
    b, t, _ = h.shape
    cq, ckv, krope, gb, gc, hv = jnp.split(h @ w_in, list(OD_SPLITS), axis=-1)
    q = (rms_norm(cq, q_a_norm) @ w_uq).reshape(b, t, C_HEADS, C_NOPE + C_ROPE)
    q_nope, q_rope = jnp.split(q, [C_NOPE], axis=-1)
    return q_nope, q_rope, rms_norm(ckv, kv_a_norm), krope, gb, gc, hv

def mla_attention(q_nope, q_rope, ckv, krope, w_ukv):
    b, s, _ = ckv.shape
    k_nope, v = jnp.split((ckv @ w_ukv).reshape(b, s, C_HEADS, C_NOPE + C_V), [C_NOPE], axis=-1)
    k = jnp.concatenate([k_nope, jnp.broadcast_to(krope[:, :, None, :], (b, s, C_HEADS, C_ROPE))], axis=-1)
    q = jnp.concatenate([q_nope, q_rope], axis=-1)
    o = block_attention(q.transpose(0, 2, 1, 3)[:, :, None], k.transpose(0, 2, 1, 3), v.transpose(0, 2, 1, 3))
    return merge_heads(o)

def short_conv(gb, gc, hv, w):
    z = gc * hv
    zp = jnp.pad(z, ((0, 0), (1, 1), (0, 0)))
    y = zp[:, :-2] * w[0] + zp[:, 1:-1] * w[1] + zp[:, 2:] * w[2]
    return gb * y

def odd_context(h, w_in, q_a_norm, kv_a_norm, w_uq, w_ukv, conv_w, w_out):
    q_nope, q_rope, ckv, krope, gb, gc, hv = odd_project(h, w_in, q_a_norm, kv_a_norm, w_uq)
    a = mla_attention(q_nope, q_rope, ckv, krope, w_ukv)
    out = jnp.concatenate([a, short_conv(gb, gc, hv, conv_w)], axis=-1) @ w_out
    return out, ckv, krope

def odd_latent(h, ckv_ctx, krope_ctx, w_in, q_a_norm, kv_a_norm, w_uq, w_ukv, conv_w, w_out):
    t = h.shape[1]
    q_nope, q_rope, ckv, krope, gb, gc, hv = odd_project(h, w_in, q_a_norm, kv_a_norm, w_uq)
    ang_r, ang_c = grid_angles(t, C_ROPE)
    q_rope = axial_rope(q_rope, ang_r[:, None], ang_c[:, None])
    krope = axial_rope(krope, ang_r, ang_c)
    a = mla_attention(q_nope, q_rope, jnp.concatenate([ckv_ctx, ckv], axis=1),
                      jnp.concatenate([krope_ctx, krope], axis=1), w_ukv)
    return jnp.concatenate([a, short_conv(gb, gc, hv, conv_w)], axis=-1) @ w_out

def ec_moe(x, w_router, w_gate, w_up, w_down):
    b, t, d = x.shape
    cap = EC_CAPACITY * t // N_EXPERTS
    logits = jnp.einsum('btd,de->bet', x, w_router, preferred_element_type=jnp.float32)
    aff = jax.nn.softmax(logits, axis=1)
    gate, idx = lax.top_k(aff, cap)
    xs = jax.vmap(lambda xb, ib: xb[ib])(x, idx)
    hid = jax.nn.silu(jnp.einsum('becd,edf->becf', xs, w_gate)) * jnp.einsum('becd,edf->becf', xs, w_up)
    y = jnp.einsum('becf,efd->becd', hid, w_down) * gate[..., None].astype(x.dtype)
    return jax.vmap(lambda yb, ib: jnp.zeros((t, d), yb.dtype).at[ib].add(yb))(y, idx)

def setup_inputs(seed: int = 0) -> dict:
    key = jax.random.key(seed)
    ks = iter(jax.random.split(key, 40))

    def nrm(shape, scale=1.0):
        return jax.random.normal(next(ks), shape, jnp.float32) * scale

    def gain(shape):
        return 1.0 + 0.01 * nrm(shape)

    D = D_MODEL
    return {
        'x_prompt': nrm((BATCH, SEQ, D)),
        'x_sample': nrm((DEC_BATCH, DEC_SEQ, D)),
        'c': nrm((DEC_BATCH, D)),
        'cache_attn_k': nrm((DEC_BATCH, N_EVEN, B_KV_HEADS, PAST_LEN, HEAD_DIM)),
        'cache_attn_v': nrm((DEC_BATCH, N_EVEN, B_KV_HEADS, PAST_LEN, HEAD_DIM)),
        'cache_mla_ckv': nrm((DEC_BATCH, N_ODD, PAST_LEN, C_KV_LORA)),
        'cache_mla_krope': nrm((DEC_BATCH, N_ODD, PAST_LEN, C_ROPE)),
        'c_ctx': nrm((D,)),
        'w_mod': nrm((DEPTH, D, 6 * D), 0.5 * D ** -0.5),
        'b_mod': nrm((DEPTH, 6 * D), 0.01),
        'norm1': gain((DEPTH, D)),
        'norm2': gain((DEPTH, D)),
        'ev_w_in': nrm((N_EVEN, D, EV_IN), D ** -0.5),
        'ev_q_norm': gain((N_EVEN, HEAD_DIM)),
        'ev_k_norm': gain((N_EVEN, HEAD_DIM)),
        'ev_w_s': nrm((N_EVEN, A_GROUPS, CHUNK, CHUNK), CHUNK ** -0.5),
        'ev_b_s': nrm((N_EVEN, A_GROUPS, CHUNK), 0.01),
        'ev_w_out': nrm((N_EVEN, EV_OUT, D), EV_OUT ** -0.5),
        'od_w_in': nrm((N_ODD, D, OD_IN), D ** -0.5),
        'od_q_a_norm': gain((N_ODD, C_Q_LORA)),
        'od_kv_a_norm': gain((N_ODD, C_KV_LORA)),
        'od_w_uq': nrm((N_ODD, C_Q_LORA, C_HEADS * (C_NOPE + C_ROPE)), C_Q_LORA ** -0.5),
        'od_w_ukv': nrm((N_ODD, C_KV_LORA, C_HEADS * (C_NOPE + C_V)), C_KV_LORA ** -0.5),
        'od_conv_w': nrm((N_ODD, D_CONV, D_WIDTH), D_CONV ** -0.5),
        'od_w_out': nrm((N_ODD, OD_OUT, D), OD_OUT ** -0.5),
        'moe_router': nrm((DEPTH, D, N_EXPERTS), D ** -0.5),
        'moe_w_gate': nrm((DEPTH, N_EXPERTS, D, EXPERT_FF), D ** -0.5),
        'moe_w_up': nrm((DEPTH, N_EXPERTS, D, EXPERT_FF), D ** -0.5),
        'moe_w_down': nrm((DEPTH, N_EXPERTS, EXPERT_FF, D), EXPERT_FF ** -0.5),
        'final_norm': gain((D,)),
    }

def reference(x_prompt, x_sample, c, cache_attn_k, cache_attn_v, cache_mla_ckv, cache_mla_krope, c_ctx,
              w_mod, b_mod, norm1, norm2, ev_w_in, ev_q_norm, ev_k_norm, ev_w_s, ev_b_s, ev_w_out,
              od_w_in, od_q_a_norm, od_kv_a_norm, od_w_uq, od_w_ukv, od_conv_w, od_w_out,
              moe_router, moe_w_gate, moe_w_up, moe_w_down, final_norm):
    xc, xl = x_prompt, x_sample
    new_k, new_v, new_ckv, new_kr = [], [], [], []
    for layer in range(DEPTH):
        sh1c, sc1c, g1c, sh2c, sc2c, g2c = modulation(c_ctx[None], w_mod[layer], b_mod[layer])
        sh1l, sc1l, g1l, sh2l, sc2l, g2l = modulation(c, w_mod[layer], b_mod[layer])
        hc = rms_norm(xc, norm1[layer]) * (1 + sc1c) + sh1c
        hl = rms_norm(xl, norm1[layer]) * (1 + sc1l) + sh1l
        i = layer // 2
        if layer % 2 == 0:
            oc, kc, vc = even_context(hc, ev_w_in[i], ev_q_norm[i], ev_k_norm[i], ev_w_s[i], ev_b_s[i], ev_w_out[i])
            ol = even_latent(hl, cache_attn_k[:, i], cache_attn_v[:, i], ev_w_in[i], ev_q_norm[i], ev_k_norm[i],
                             ev_w_s[i], ev_b_s[i], ev_w_out[i])
            new_k.append(kc)
            new_v.append(vc)
        else:
            oc, ckv_c, kr_c = odd_context(hc, od_w_in[i], od_q_a_norm[i], od_kv_a_norm[i], od_w_uq[i],
                                          od_w_ukv[i], od_conv_w[i], od_w_out[i])
            ol = odd_latent(hl, cache_mla_ckv[:, i], cache_mla_krope[:, i], od_w_in[i], od_q_a_norm[i],
                            od_kv_a_norm[i], od_w_uq[i], od_w_ukv[i], od_conv_w[i], od_w_out[i])
            new_ckv.append(ckv_c)
            new_kr.append(kr_c)
        xc = xc + g1c * oc
        xl = xl + g1l * ol
        hc = rms_norm(xc, norm2[layer]) * (1 + sc2c) + sh2c
        hl = rms_norm(xl, norm2[layer]) * (1 + sc2l) + sh2l
        xc = xc + g2c * ec_moe(hc, moe_router[layer], moe_w_gate[layer], moe_w_up[layer], moe_w_down[layer])
        xl = xl + g2l * ec_moe(hl, moe_router[layer], moe_w_gate[layer], moe_w_up[layer], moe_w_down[layer])
    y_prompt = rms_norm(xc, final_norm)
    y_sample = rms_norm(xl, final_norm)
    return (y_prompt, y_sample, jnp.stack(new_k, axis=1), jnp.stack(new_v, axis=1),
            jnp.stack(new_ckv, axis=1), jnp.stack(new_kr, axis=1))


_drawn_inputs = setup_inputs


def setup_inputs(seed=0):
    import zlib

    import numpy as np

    out = dict(_drawn_inputs(seed))
    spreads = {}
    factors = {'cache_attn_k': 7.405,
     'cache_attn_v': 6.165,
     'cache_mla_ckv': 8.0,
     'cache_mla_krope': 8.0,
     'b_mod': 3.3,
     'norm1': 5.597,
     'norm2': 8.0,
     'ev_q_norm': 8.0,
     'ev_k_norm': 5.826,
     'ev_b_s': 8.0,
     'od_q_a_norm': 64.0,
     'od_kv_a_norm': 34.787,
     'final_norm': 34.051}
    for name, (base, spread) in spreads.items():
        noise = np.random.default_rng([zlib.crc32(name.encode()), seed]).standard_normal(out[name].shape)
        drawn = base * np.exp(spread * noise) if base else spread * noise
        out[name] = __import__('jax').numpy.asarray(drawn.astype(out[name].dtype))
    for name, factor in factors.items():
        out[name] = (out[name] * factor).astype(out[name].dtype)
    return out
```

```python
from contextlib import ExitStack

import numpy as np

import concourse.bass as bass
from concourse import mybir

F32 = mybir.dt.float32
U32 = mybir.dt.uint32
ALU = mybir.AluOpType
ACT = mybir.ActivationFunctionType
AX = mybir.AxisListType

P = 128
D = 1024
KD = D // P
NL, NC = 512, 128
T = NL + NC
NT = T // P
LAYERS = 2
HD = 64
HEADS, KV = 8, 2
GRID_W = 64
EPS = 1e-6
EV_IN, OD_IN = 1792, 1952
AW = 512
QL, KVL, ROPE, NOPE = 256, 128, 32, 64
QKC = NOPE + ROPE
KEYS = P + T
E = 16
CAP_L, CAP_C = 2 * NL // E, 2 * NC // E
CAP = CAP_L + CAP_C
FF = 512
KF = FF // P
MODC = 512
LAT, CTX = slice(0, NL), slice(NL, T)
GROUPS = (LAT, CTX)

C_ID, C_ONED, C_BLK, C_ONE2, C_ONE1, C_PERM, C_PERMO, C_SEL = 0, 128, 256, 384, 512, 640, 768, 800
C_END = 800 + 512

R_C, R_CTX, R_N1, R_N2, R_FIN, R_CONV, R_QA, R_KVA, R_EVQ, R_EVK, R_END = 0, 8, 16, 32, 48, 56, 68, 70, 71, 72, 73

STEPS = [(h, t) for h in range(HEADS) for t in range(NT)]


class PsumPlan:

    def __init__(self):
        self.full, self.freed, self.reader, self.banks, self.order = {}, {}, {}, {}, []
        self.count = {"act": 0, "dve": 0}

    def add(self, name, banks, reader):
        assert name not in self.full
        self.order.append(name)
        self.full[name] = len(self.order)
        self.count[reader] += 1
        self.freed[name] = self.count[reader]
        self.reader[name], self.banks[name] = reader, banks

    def before(self, name):
        at, found = self.full[name] - 1, []
        for b in self.banks[name]:
            for other in reversed(self.order[:at]):
                if b in self.banks[other]:
                    if other not in found:
                        found.append(other)
                    break
        return found


def projections(kind, tiles):
    return [((kind, m), m) for m in range(tiles)] + [((kind, "ctx"), None)]


def plan_psum():
    p = PsumPlan()
    ring = [0]

    def one(name, reader, banks=1):
        b = ring[0] % 8
        if b + banks > 8:
            b = 0
        p.add(name, list(range(b, b + banks)), reader)
        ring[0] = b + banks

    one("cols", "act"), one("bias cols", "act")
    for k in range(KD):
        one(("x", k), "dve")
    one(("x", "ctx0"), "dve"), one(("x", "ctx1"), "dve")
    for c in range(LAYERS * 6 * D // MODC):
        one(("mod", c), "dve")
    for L in range(LAYERS):
        one((L, "norm", 0), "dve", 2)
        if L == 0:
            one("wsT0", "act"), one("wsT1", "act")
            for t in range(NT):
                one(("va", t), "act")
            for g in range(4):
                one(("s", g), "dve")
            one(("s", "ctx"), "dve")
            for n, _ in projections("u", 4):
                one(n, "dve")
            for n, _ in projections("q", 4):
                one(n, "act")
            one(("k", 0), "act"), one(("k", "ctx"), "act")
            one("v lat", "act"), one("v ctx", "act")
            one("cache k", "act")
            for m in range(5):
                one(("qk norm", m), "dve", 2)
                one(("qk rot", m), "dve")
            one("new k", "dve")
        else:
            for kind, reader in (("gc", "act"), ("hv", "dve"), ("gb", "dve")):
                for n, _ in projections(kind, 4):
                    one(n, reader)
            for n, _ in projections("cq", 2):
                one(n, "act")
            one(("ckv", 0), "act"), one(("ckv", "ctx"), "act")
            one(("kr", 0), "act"), one(("kr", "ctx"), "act")
            one("cache ckv", "act"), one("cache kr", "act")
            one("cq norm", "dve", 2), one("ckv norm", "dve", 2)
            one("kr rot", "dve")
            one("new ckv", "dve"), one("new kr", "dve")
            for t in range(KEYS // P):
                one(("v", t), "act")

        def prepare(h):
            if L == 1:
                if h % 2 == 0:
                    p.add(("kn", h // 2), [4, 5], "act")
                p.add(("uq", h), [4, 5], "act")
                p.add(("uq rot", h), [4], "dve")

        prepare(0)
        p.add((L, "S", 0), [0, 1], "act")
        for i, (h, t) in enumerate(STEPS):
            if i + 1 < len(STEPS):
                if t == NT - 1:
                    prepare(h + 1)
                b = 2 * ((i + 1) % 2)
                p.add((L, "S", i + 1), [b, b + 1], "act")
            if i >= 1:
                values_after(p, L, i - 1)
            p.add((L, "T", i), [4, 5], "act")
        values_after(p, L, len(STEPS) - 1)
        for n, _ in projections((L, "out"), KD):
            one(n, "dve") if n[1] != "ctx" else one((n[0], "ctx0"), "dve")
        one(((L, "out"), "ctx1"), "dve")
        one((L, "norm", 1), "dve", 2)
        one((L, "logits"), "dve")
        one((L, "aff"), "act"), one((L, "aff ctx"), "act")
        for t in range(NT):
            one((L, "h", t), "act", 2)
        one((L, "gates"), "act")
        for k in range(KD):
            one((L, "moe", k), "dve")
        one((L, "moe", "ctx0"), "dve"), one((L, "moe", "ctx1"), "dve")
    one((LAYERS, "norm", 0), "dve", 2)
    for t in range(NT):
        one(("y", t), "act", 2)
    return p


def values_after(p, L, i):
    h, t = STEPS[i]
    if t == NT - 2:
        p.add((L, "O", h), [7], "dve")
    if t == NT - 1:
        p.add((L, "Oc", h), [6], "dve")


def trunk(nc, a, out):
    plan = plan_psum()
    with ExitStack() as ctx:
        def sb(name, n):
            return ctx.enter_context(nc.sbuf_tensor(name, [P, n], F32))

        def sem(name):
            return ctx.enter_context(nc.semaphore(name))

        xT_ = sb("xT", KD * T)
        hT_ = sb("hT", KD * T)
        wts = sb("wts", 24576)
        cst = sb("cst", C_END)
        cs = sb("cs", 2 * NL)
        cols = sb("cols", R_END + 1)
        bcol = sb("bcol", 96)
        sT_ = sb("sT", 2 * KD)
        mod_ = sb("mod", LAYERS * 48 * 2)
        amul_ = sb("amul", LAYERS * 2 * 2 * KD)
        bs = sb("bs", P)
        router_ = sb("router", LAYERS * KD * E)
        stat = sb("stat", 16)
        small = sb("small", 320)
        arena = sb("arena", 14336)
        psum = ctx.enter_context(nc.psum_tensor("psum", [P, 8, 512], F32))

        h_dram = [nc.dram_tensor(f"h_dram{L}", (T, D), F32).ap() for L in range(LAYERS)]
        acc_dram = [nc.dram_tensor(f"acc_dram{L}", (T, D), F32).ap() for L in range(LAYERS)]

        def v3(t, at, n, m):
            return t[:, at:at + n * m].rearrange("p (n m) -> p n m", n=n)

        xT, hT = v3(xT_, 0, KD, T), v3(hT_, 0, KD, T)
        xtok = v3(hT_, 0, NT, D)
        ident, ones_d, blk64 = cst[:, C_ID:C_ID + P], cst[:, C_ONED:C_ONED + P], cst[:, C_BLK:C_BLK + P]
        ones_ql, ones_kvl = cst[:, C_ONE2:C_ONE2 + P], cst[:, C_ONE1:C_ONE1 + P]
        perm, permo = cst[:, C_PERM:C_PERM + P], cst[64:96, C_PERMO:C_PERMO + 32]
        sel = cst[0:8, C_SEL:C_SEL + 512].rearrange("p (g m) -> p g m", g=4)
        rope_c, rope_s = cs[:, 0:NL], cs[:, NL:2 * NL]
        sT = v3(sT_, 0, KD, 2)
        mod = mod_[:, :].rearrange("p (l j k g) -> p l j k g", l=LAYERS, j=6, k=KD)
        mod_blocks = mod_[:, :].rearrange("p (c g) -> p c g", g=2)
        amul = amul_[:, :].rearrange("p (l w k g) -> p l w k g", l=LAYERS, w=2, k=KD)
        router = [v3(router_, KD * E * L, KD, E) for L in range(LAYERS)]
        w_in = {0: v3(wts, 0, KD, EV_IN), 1: v3(wts, 0, KD, OD_IN)}
        w_out = v3(wts, 16384, KD, D)
        kr = wts[64:96, 15616:15616 + KEYS]
        wg = [v3(wts, 12288 * s, KD, FF) for s in range(2)]
        wu = [v3(wts, 12288 * s + 4096, KD, FF) for s in range(2)]
        wd = [v3(wts, 12288 * s + 8192, KF, D) for s in range(2)]
        wmod = [v3(wts, 4096 * s, KD, MODC) for s in range(6)]
        sq = [arena[:, T * s:T * s + T] for s in range(2)]
        prob = sq
        rstd = arena[:, 1280:1920]
        var = sq[1]
        qT = v3(arena, 1920, 4, T)
        kT = arena[:, 4480:4480 + KEYS]
        kdup = v3(arena, 5248, 2, KEYS)
        wsraw = v3(arena, 5248, 8, P)
        vtok_e = v3(arena, 6784, 6, P)
        va = v3(arena, 7552, NT, AW)
        gated = v3(arena, 10112, 4, T)
        wsT = v3(arena, 12672, 8, P)
        tmp_e = arena[:, 13696:13696 + NL]
        yT = v3(arena, 1920, 4, T)
        zT = v3(arena, 4480, 4, T)
        cq = v3(arena, 7040, 2, T)
        ckv = arena[:, 8320:8320 + KEYS]
        qh = [arena[:, 9088:9088 + T], rstd]
        vtok_o = v3(arena, 9728, 6, AW)
        w_uq = v3(arena, 12800, 2, HEADS * QKC)
        kh = [hT_[:, 2560 + KEYS * s:2560 + KEYS * (s + 1)] for s in range(2)]
        w_uk, w_uv = hT_[:, 4096:4608], hT_[:, 4608:5120]
        oT = v3(hT_, 0, 4, T)
        tmp_o = arena[:, 4480 + 1920:4480 + 1920 + NL]
        pT = {0: [v3(arena, 7552 + T * s, NT, P) for s in range(3)],
              1: [v3(arena, 4480 + T * s, NT, P) for s in range(3)]}
        tmp = {0: tmp_e, 1: tmp_o}
        htok = [arena[:, D * s:D * s + D] for s in range(2)]
        xs = [arena[0:CAP, 2048 + D * s:2048 + D * s + D] for s in range(2)]
        xsT = [v3(arena, 4096 + KD * CAP * s, KD, CAP) for s in range(2)]
        sig = [v3(arena, 5376 + KF * CAP * s, KF, CAP) for s in range(2)]
        hid = [v3(arena, 6016 + KF * CAP * s, KF, CAP) for s in range(2)]
        ysb = [arena[0:CAP, 6656 + D * s:6656 + D * s + D] for s in range(2)]
        aff = v3(arena, 8704, NT, E)
        aff_e = v3(arena, 8784, NT, E)
        work = arena[0:E, 8864:8864 + T]
        vals = arena[0:E, 9504:9504 + CAP]
        idx = arena[0:E, 9584:9584 + CAP].bitcast(U32)
        idxf = arena[0:E, 9664:9664 + CAP]
        gates = arena[0:CAP, 9744:9744 + E]
        slots = arena[0:CAP, 9760:9760 + E].bitcast(U32)
        rowmax, rowsum = arena[:, 9776:9781], arena[:, 9781:9786]
        zeros = arena[:, 10240:10240 + D]
        ytok = [arena[:, 2048 + D * s:2048 + D * s + D] for s in range(2)]

        consts_in, rows_in, x_in, zeroed, zero_out = (sem(n) for n in ("consts_in", "rows_in", "x_in", "zeroed", "zero_out"))
        psum_full = sem("psum_full")
        freed = {"act": sem("freed_act"), "dve": sem("freed_dve")}
        silu_ready, silu_exp = sem("silu_ready"), sem("silu_exp")
        wmod_in = [sem(f"wmod_in{s}") for s in range(6)]
        win_in, wout_in, cs_in, attn_w_in, ukv_in = (sem(n) for n in ("win_in", "wout_in", "cs_in", "attn_w_in", "ukv_in"))
        router_in = sem("router_in")
        log_done = sem("log_done")
        root_done = sem("root_done")
        sq_ready, sq_used, h_scaled, h_ready = (sem(n) for n in ("sq_ready", "sq_used", "h_scaled", "h_ready"))
        proj_norm = sem("proj_norm")
        roped = sem("roped")
        kdup_ready = sem("kdup_ready")
        kr_copied = sem("kr_copied")
        new_out = sem("new_out")
        s_max, s_prob, s_norm = sem("s_max"), sem("s_prob"), sem("s_norm")
        aff_exp, aff_done, topk_done = (sem(n) for n in ("aff_exp", "aff_done", "topk_done"))
        h_out = [sem(f"h_out{s}") for s in range(2)]
        wg_in = [sem(f"wg_in{s}") for s in range(2)]
        wu_in = [sem(f"wu_in{s}") for s in range(2)]
        wd_in = [sem(f"wd_in{s}") for s in range(2)]
        gathered = [sem(f"gathered{s}") for s in range(2)]
        xsT_full, xsT_ready, gu_full, sig_exp, sig_step, hid_ready, y_full, y_ready = (
            sem(n) for n in ("xsT_full", "xsT_ready", "gu_full", "sig_exp", "sig_step", "hid_ready", "y_full", "y_ready"))
        scattered = sem("scattered")
        acc_in = sem("acc_in")
        y_out = [sem(f"y_out{s}") for s in range(2)]
        dve_step, act_step = sem("dve_step"), sem("act_step")

        def filled(eng, name):
            eng.wait_ge(psum_full, plan.full[name])

        def emptied(eng, name):
            eng.wait_ge(freed[plan.reader[name]], plan.freed[name])

        def bank(name, i=0):
            return psum[:, plan.banks[name][i], :]

        def pair(name, rows=P, n=T):
            b = plan.banks[name][0]
            return psum[0:rows, b:b + 2, :].rearrange("p b n -> p (b n)")[:, 0:n]

        def x_last(L, norm):
            if L == 0 and norm == 0:
                return ("x", "ctx1")
            return (L - 1, "moe", "ctx1") if norm == 0 else ((L, "out"), "ctx1")

        block = ctx.enter_context(nc.Block())

        @block.sync
        def _(sp):
            sp.dma_start(cst[:, :], a["const"]).then_inc(consts_in, 16)
            rows = small[0:96, 0:P]
            rows2 = small[0:96, P:2 * P]

            def row(at, src, n):
                sp.dma_start(small[at:at + n, 0:P], src).then_inc(rows_in, 16)

            row(R_C, a["c"].rearrange("b (k p) -> (b k) p", p=P), 8)
            row(R_CTX, a["c_ctx"].rearrange("(k p) -> k p", p=P), 8)
            row(R_N1, a["norm1"].rearrange("l (k p) -> (l k) p", p=P), 16)
            row(R_N2, a["norm2"].rearrange("l (k p) -> (l k) p", p=P), 16)
            row(R_FIN, a["final_norm"].rearrange("(k p) -> k p", p=P), 8)
            row(R_CONV, a["od_conv_w"].rearrange("l w (k p) -> (l w k) p", p=P), 12)
            row(R_QA, a["od_q_a_norm"].rearrange("l (k p) -> (l k) p", p=P), 2)
            row(R_KVA, a["od_kv_a_norm"], 1)
            for r, n in ((R_EVQ, "ev_q_norm"), (R_EVK, "ev_k_norm")):
                for half in range(2):
                    sp.dma_start(small[r:r + 1, HD * half:HD * half + HD], a[n]).then_inc(rows_in, 16)
            sp.dma_start(rows2, a["b_mod"].rearrange("l (k p) -> (l k) p", p=P)).then_inc(rows_in, 16)
            sp.dma_start(xtok[:, 0:4, :], a["x_sample"].rearrange("b (t p) d -> p (b t) d", p=P)).then_inc(x_in, 16)
            sp.dma_start(xtok[:, 4, :], a["x_prompt"][0]).then_inc(x_in, 16)
            for L in range(LAYERS):
                sp.dma_start(router[L], a["moe_router"][L].rearrange("(k p) e -> p k e", p=P)).then_inc(router_in, 16)
            chunks = 6 * D // MODC
            for c in range(LAYERS * chunks):
                if c >= 6:
                    filled(sp, ("mod", c - 6))
                L, j = divmod(c, chunks)
                sp.dma_start(wmod[c % 6], a["w_mod"][L].rearrange("(k p) n -> p k n", p=P)[:, :, MODC * j:MODC * (j + 1)])\
                    .then_inc(wmod_in[c % 6], 16)
            for L in range(LAYERS):
                if L == 0:
                    sp.dma_start(bs[0:8, :], a["ev_b_s"][0]).then_inc(attn_w_in, 16)
                    sp.dma_start(wsraw, a["ev_w_s"][0].rearrange("g p q -> p g q")).then_inc(attn_w_in, 16)
                    filled(sp, ("mod", LAYERS * chunks - 1))
                else:
                    sp.wait_ge(y_full, E * L)
                w = a["ev_w_in"] if L == 0 else a["od_w_in"]
                sp.dma_start(w_in[L], w[0].rearrange("(k p) n -> p k n", p=P)).then_inc(win_in, 16)
                wo = a["ev_w_out"] if L == 0 else a["od_w_out"]
                sp.dma_start(w_out, wo[0].rearrange("(k p) n -> p k n", p=P)).then_inc(wout_in, 16)
                if L == 0:
                    sp.dma_start(cs[:, :], a["rope_even"]).then_inc(cs_in, 16)
                    filled(sp, "bias cols")
                    sp.dma_start(small[:, 0:P].rearrange("p (g d) -> p g d", g=KV),
                                 a["cache_attn_k"][0, 0].rearrange("g s d -> s g d")).then_inc(attn_w_in, 16)
                    sp.dma_start(vtok_e[:, 0, :].rearrange("p (g d) -> p g d", g=KV),
                                 a["cache_attn_v"][0, 0].rearrange("g s d -> s g d")).then_inc(attn_w_in, 16)
                    emptied(sp, "new k")
                    sp.dma_start(out["new_k"][0, 0].rearrange("g s d -> s g d"),
                                 small[:, P:2 * P].rearrange("p (g d) -> p g d", g=KV)).then_inc(new_out, 16)
                    emptied(sp, "v ctx")
                    sp.dma_start(out["new_v"][0, 0].rearrange("g s d -> s g d"),
                                 vtok_e[:, 5, :].rearrange("p (g d) -> p g d", g=KV)).then_inc(new_out, 16)
                else:
                    sp.dma_start(cs[64:96, :], a["rope_odd"]).then_inc(cs_in, 16)
                    sp.wait_ge(new_out, 32)
                    sp.dma_start(small[:, 0:KVL], a["cache_mla_ckv"][0, 0]).then_inc(attn_w_in, 16)
                    sp.dma_start(small[:, KVL:KVL + ROPE], a["cache_mla_krope"][0, 0]).then_inc(attn_w_in, 16)
                    sp.dma_start(w_uq, a["od_w_uq"][0].rearrange("(k p) n -> p k n", p=P)).then_inc(attn_w_in, 16)
                    filled(sp, ("kr", "ctx"))
                    ukv = a["od_w_ukv"][0].rearrange("r (h c) -> r h c", h=HEADS)
                    sp.dma_start(w_uk.rearrange("p (h c) -> p h c", h=HEADS), ukv[:, :, 0:NOPE]).then_inc(ukv_in, 16)
                    sp.dma_start(w_uv.rearrange("p (h c) -> p h c", h=HEADS), ukv[:, :, NOPE:NOPE + HD]).then_inc(ukv_in, 16)
                    emptied(sp, "new kr")
                    sp.dma_start(out["new_ckv"][0, 0], small[:, 160:160 + KVL]).then_inc(new_out, 16)
                    sp.dma_start(out["new_kr"][0, 0], small[:, 288:288 + ROPE]).then_inc(new_out, 16)
                filled(sp, ((L, "out"), "ctx1"))
                wgd, wud = (a[n][L].rearrange("e (k p) f -> e p k f", p=P) for n in ("moe_w_gate", "moe_w_up"))
                wdd = a["moe_w_down"][L].rearrange("e (k p) n -> e p k n", p=P)

                def expert(s, e):
                    sp.dma_start(wg[s], wgd[e]).then_inc(wg_in[s], 16)
                    sp.dma_start(wu[s], wud[e]).then_inc(wu_in[s], 16)
                    sp.dma_start(wd[s], wdd[e]).then_inc(wd_in[s], 16)

                expert(0, 0)
                expert(1, 1)
                for t in range(NT):
                    emptied(sp, (L, "h", t))
                    sp.dma_start(h_dram[L][P * t:P * t + P, :], htok[t % 2]).then_inc(h_out[t % 2], 16)
                with sp.Fori(0, E // 2 - 1) as i:
                    for s in range(2):
                        sp.wait_ge(gu_full, i * 2 + (E * L + s + 1))
                        sp.dma_start(wg[s], wgd[bass.ds(i * 2 + (s + 2), 1), :, :, :].rearrange("o p k f -> p (o k) f")).then_inc(wg_in[s], 16)
                        sp.dma_start(wu[s], wud[bass.ds(i * 2 + (s + 2), 1), :, :, :].rearrange("o p k f -> p (o k) f")).then_inc(wu_in[s], 16)
                        sp.wait_ge(y_full, i * 2 + (E * L + s + 1))
                        sp.dma_start(wd[s], wdd[bass.ds(i * 2 + (s + 2), 1), :, :, :].rearrange("o p k n -> p (o k) n")).then_inc(wd_in[s], 16)
                sp.wait_ge(scattered, 16 * E * (L + 1))
                sp.dma_start(xtok, acc_dram[L].rearrange("(t p) d -> p t d", p=P)).then_inc(acc_in, 16)
            for t in range(NT):
                emptied(sp, ("y", t))
                dst = out["y_sample"][0, P * t:P * t + P, :] if t < NT - 1 else out["y_prompt"][0]
                sp.dma_start(dst, ytok[t % 2]).then_inc(y_out[t % 2], 16)
            sp.wait_ge(y_out[0], 16 * 3)
            sp.wait_ge(y_out[1], 16 * 2)
            sp.wait_ge(new_out, 16 * 4)

        @block.gpsimd
        def _(pool):
            pool.memset(zeros, 0.0).then_inc(zeroed, 1)
            pool.wait_ge(zeroed, 1)
            for L in range(LAYERS):
                for t in range(NT):
                    pool.dma_start(acc_dram[L][P * t:P * t + P, :], zeros).then_inc(zero_out, 16)
            pool.wait_ge(zero_out, 16 * LAYERS * NT)

            for L in range(LAYERS):
                emptied(pool, (L, "gates"))
                pool.wait_ge(h_out[0], 16 * 3 * (L + 1))
                pool.wait_ge(h_out[1], 16 * 2 * (L + 1))

                def gather(e):
                    if e >= 2:
                        pool.wait_ge(xsT_full, E * L + e - 1)
                    pool.indirect_dma_start(xs[e % 2], None, h_dram[L], bass.IndirectOffsetOnAxis(slots[:, e:e + 1], 0))\
                        .then_inc(gathered[e % 2], 16)

                def scatter(e):
                    pool.wait_ge(y_ready, E * L + e + 1)
                    if e + L:
                        pool.wait_ge(scattered, 16 * (E * L + e))
                    pool.indirect_dma_start(acc_dram[L], bass.IndirectOffsetOnAxis(slots[:, e:e + 1], 0), ysb[e % 2], None,
                                            compute_op=ALU.add).then_inc(scattered, 16)

                gather(0)
                gather(1)
                for e in range(E):
                    if e + 2 < E:
                        gather(e + 2)
                    scatter(e)

        @block.tensor
        def _(pe):
            squared = [0]

            def begin(name):
                for other in plan.before(name):
                    emptied(pe, other)

            def mm(o, w, x, first, last):
                return pe.matmul(o, w, x, start=first, stop=last, skip_group_check=True)

            def norm_sums(name, weights, tiles=KD):
                begin(name)
                for k in range(tiles):
                    squared[0] += 1
                    pe.wait_ge(sq_ready, squared[0])
                    mm(bank(name, 0), weights, sq[k % 2][:, LAT], k == 0, k == tiles - 1)
                    ins = mm(bank(name, 1)[:, 0:NC], weights, sq[k % 2][:, CTX], k == 0, k == tiles - 1)
                    ins.then_inc(sq_used if k < tiles - 1 else psum_full, 1)

            def project(kind, tiles, w, at, rhs, kt=KD, ctx_banks=1):
                for m in range(tiles):
                    begin((kind, m))
                    for k in range(kt):
                        ins = mm(bank((kind, m)), w[:, k, at + P * m:at + P * m + P], rhs(k)[:, LAT], k == 0, k == kt - 1)
                    ins.then_inc(psum_full, 1)
                per = -(-tiles // ctx_banks)
                for b in range(ctx_banks):
                    name = (kind, "ctx" if ctx_banks == 1 else f"ctx{b}")
                    begin(name)
                    for j in range(per):
                        m = b * per + j
                        for k in range(kt):
                            ins = mm(bank(name)[:, P * j:P * j + P], w[:, k, at + P * m:at + P * m + P], rhs(k)[:, CTX],
                                     k == 0, k == kt - 1)
                    ins.then_inc(psum_full, 1)

            def to_features(kind, src):
                for k in range(KD):
                    begin((*kind, k))
                    for t in range(4):
                        ins = pe.transpose(bank((*kind, k))[:, P * t:P * t + P], src[:, t, P * k:P * k + P], ident)
                    ins.then_inc(psum_full, 1)
                for b in range(2):
                    name = (*kind, f"ctx{b}")
                    begin(name)
                    for j in range(4):
                        k = 4 * b + j
                        ins = pe.transpose(bank(name)[:, P * j:P * j + P], src[:, 4, P * k:P * k + P], ident)
                    ins.then_inc(psum_full, 1)

            pe.wait_ge(consts_in, 16)
            pe.wait_ge(rows_in, 16 * 13)
            pe.transpose(bank("cols")[:, 0:R_END], small[0:R_END, 0:P], ident[0:R_END, 0:R_END]).then_inc(psum_full, 1)
            pe.transpose(bank("bias cols")[:, 0:96], small[0:96, P:2 * P], ident[0:96, 0:96]).then_inc(psum_full, 1)
            pe.wait_ge(x_in, 32)
            to_features(("x",), xtok)
            pe.wait_ge(silu_ready, 1)
            for c in range(LAYERS * 6 * D // MODC):
                begin(("mod", c))
                pe.wait_ge(wmod_in[c % 6], 16 * (c // 6 + 1))
                for b in range(MODC // P):
                    for k in range(KD):
                        ins = mm(bank(("mod", c))[:, 2 * b:2 * b + 2], wmod[c % 6][:, k, P * b:P * b + P], sT[:, k, :],
                                 k == 0, k == KD - 1)
                ins.then_inc(psum_full, 1)

            for L in range(LAYERS):
                norm_sums((L, "norm", 0), ones_d)
                W = w_in[L]

                def h(k):
                    return hT[:, k, :]

                pe.wait_ge(win_in, 16 * (L + 1))
                pe.wait_ge(h_ready, KD * (2 * L + 1))
                if L == 0:
                    pe.wait_ge(attn_w_in, 16 * 4)
                    for j in range(2):
                        begin(f"wsT{j}")
                        for g in range(4):
                            ins = pe.transpose(bank(f"wsT{j}")[:, P * g:P * g + P], wsraw[:, 4 * j + g, :], ident)
                        ins.then_inc(psum_full, 1)
                    for t in range(NT):
                        begin(("va", t))
                        for k in range(KD):
                            ins = mm(bank(("va", t)), hT[:, k, P * t:P * t + P], W[:, k, AW:2 * AW], k == 0, k == KD - 1)
                        ins.then_inc(psum_full, 1)
                    emptied(pe, ("va", NT - 1))
                    for g in range(4):
                        begin(("s", g))
                        b_rows = bs[0:8, :].rearrange("p (o q) -> p o q", o=1).to_broadcast([8, 4, P])
                        mm(bank(("s", g)).rearrange("p (o q) -> p o q", o=4), sel[:, g, :], b_rows, True, False)
                        for t in range(4):
                            for j in range(2):
                                ins = mm(bank(("s", g))[64 * j:64 * j + 64, P * t:P * t + P],
                                         va[:, t, P * g + 64 * j:P * g + 64 * j + 64], wsT[:, 2 * g + j, :], False, t == 3)
                        ins.then_inc(psum_full, 1)
                    begin(("s", "ctx"))
                    for g in range(4):
                        mm(bank(("s", "ctx"))[:, P * g:P * g + P], sel[:, g, :], bs[0:8, :], g == 0, False)
                        for j in range(2):
                            ins = mm(bank(("s", "ctx"))[64 * j:64 * j + 64, P * g:P * g + P],
                                     va[:, 4, P * g + 64 * j:P * g + 64 * j + 64], wsT[:, 2 * g + j, :], False, g == 3)
                    ins.then_inc(psum_full, 1)
                    project("u", 4, W, 0, h)
                    project("q", 4, W, 2 * AW, h)
                    project("k", 1, W, 3 * AW, h)
                    for name, tiles in (("v lat", range(4)), ("v ctx", [4])):
                        begin(name)
                        for j, t in enumerate(tiles):
                            for k in range(KD):
                                ins = mm(bank(name)[:, P * j:P * j + P], hT[:, k, P * t:P * t + P], W[:, k, EV_IN - P:EV_IN],
                                         k == 0, k == KD - 1)
                        ins.then_inc(psum_full, 1)
                    begin("cache k")
                    pe.transpose(bank("cache k")[:, 0:P], small[:, 0:P], ident).then_inc(psum_full, 1)
                    pe.wait_ge(cs_in, 16)
                    for m in range(5):
                        norm_sums(("qk norm", m), blk64, 1)
                        pe.wait_ge(proj_norm, m + 1)
                        src = qT[:, m, LAT] if m < 4 else kT[:, P:P + NL]
                        begin(("qk rot", m))
                        mm(bank(("qk rot", m)), perm, src, True, True).then_inc(psum_full, 1)
                    begin("new k")
                    pe.transpose(bank("new k")[:, 0:P], kT[:, P + NL:KEYS], ident).then_inc(psum_full, 1)
                    pe.wait_ge(kdup_ready, 4)
                    pe.wait_ge(roped, 5)
                else:
                    project("gc", 4, W, QL + KVL + ROPE + AW, h)
                    project("hv", 4, W, QL + KVL + ROPE + 2 * AW, h)
                    project("gb", 4, W, QL + KVL + ROPE, h)
                    project("cq", 2, W, 0, h)
                    project("ckv", 1, W, QL, h)
                    for name, grp, n in ((("kr", 0), LAT, NL), (("kr", "ctx"), CTX, NC)):
                        begin(name)
                        for k in range(KD):
                            ins = mm(bank(name)[64:96, 0:n], W[:, k, QL + KVL:QL + KVL + ROPE], hT[:, k, grp], k == 0, k == KD - 1)
                        ins.then_inc(psum_full, 1)
                    pe.wait_ge(attn_w_in, 16 * 7)
                    begin("cache ckv")
                    pe.transpose(bank("cache ckv")[:, 0:P], small[:, 0:KVL], ident).then_inc(psum_full, 1)
                    begin("cache kr")
                    pe.transpose(bank("cache kr")[0:ROPE, 0:P], small[:, KVL:KVL + ROPE], ident).then_inc(psum_full, 1)
                    norm_sums("cq norm", ones_ql, 2)
                    norm_sums("ckv norm", ones_kvl, 1)
                    pe.wait_ge(cs_in, 32)
                    emptied(pe, ("kr", "ctx"))
                    begin("kr rot")
                    mm(bank("kr rot")[64:96, :], permo, kr[:, P:P + NL], True, True).then_inc(psum_full, 1)
                    pe.wait_ge(proj_norm, 7)
                    begin("new ckv")
                    pe.transpose(bank("new ckv")[:, 0:P], ckv[:, P + NL:KEYS], ident).then_inc(psum_full, 1)
                    begin("new kr")
                    pe.transpose(bank("new kr")[:, 0:ROPE], kr[:, P + NL:KEYS], ident[64:96, 64:96]).then_inc(psum_full, 1)
                    pe.wait_ge(ukv_in, 32)
                    emptied(pe, "cache ckv")
                    for t in range(KEYS // P):
                        begin(("v", t))
                        mm(bank(("v", t)), ckv[:, P * t:P * t + P], w_uv, True, True).then_inc(psum_full, 1)

                def prepare(hh):
                    if L == 0:
                        return
                    if hh % 2 == 0:
                        name = ("kn", hh // 2)
                        begin(name)
                        kcols = w_uk[:, NOPE * hh:NOPE * hh + P]
                        mm(bank(name, 0), kcols, ckv[:, 0:512], True, True)
                        mm(bank(name, 1)[:, 0:KEYS - 512], kcols, ckv[:, 512:KEYS], True, True).then_inc(psum_full, 1)
                    name = ("uq", hh)
                    begin(name)
                    for b, grp, n in ((0, LAT, NL), (1, CTX, NC)):
                        for k in range(2):
                            ins = mm(bank(name, b)[0:QKC, 0:n], w_uq[:, k, QKC * hh:QKC * hh + QKC], cq[:, k, grp], k == 0, k == 1)
                    ins.then_inc(psum_full, 1)
                    emptied(pe, name)
                    begin(("uq rot", hh))
                    mm(bank(("uq rot", hh))[64:96, :], permo, qh[hh % 2][64:96, LAT], True, True).then_inc(psum_full, 1)

                def scores(i):
                    hh, t = STEPS[i]
                    name = (L, "S", i)
                    begin(name)
                    q_at = P * t
                    if L == 0:
                        r = slice(64 * (hh % 2), 64 * (hh % 2) + 64)
                        q, kk = qT[r, hh // 2, q_at:q_at + P], kdup[r, hh // 4, :]
                    else:
                        if t == 0:
                            pe.wait_ge(roped, 5 + 1 + hh + 1)
                            emptied(pe, ("kn", hh // 2))
                            pe.wait_ge(kr_copied, 2)
                        q, kk = qh[hh % 2][0:QKC, q_at:q_at + P], kh[hh % 2][0:QKC, :]
                    if t < 4:
                        mm(bank(name, 0), q, kk[:, 0:512], True, True)
                        mm(bank(name, 1)[:, 0:P], q, kk[:, 512:P + NL], True, True).then_inc(psum_full, 1)
                    else:
                        mm(bank(name, 0)[:, 0:P], q, kk[:, P + NL:KEYS], True, True).then_inc(psum_full, 1)

                def turn(i):
                    hh, t = STEPS[i]
                    name = (L, "T", i)
                    begin(name)
                    pe.wait_ge(s_norm, len(STEPS) * L + i + 1)
                    for kt in range(5 if t < 4 else 1):
                        ins = pe.transpose(pair(name)[:, P * kt:P * kt + P], prob[i % 2][:, P * kt:P * kt + P], ident)
                    ins.then_inc(psum_full, 1)

                def values(i):
                    hh, t = STEPS[i]
                    name = (L, "O" if t < 4 else "Oc", hh)
                    if t in (0, 4):
                        begin(name)
                    emptied(pe, (L, "T", i))
                    r = slice(64 * (hh % 2), 64 * (hh % 2) + 64)
                    tiles = list(range(5)) if t < 4 else [5]
                    o = bank(name)[r, P * t:P * t + P] if t < 4 else bank(name)[r, 0:P]
                    for n, kt in enumerate(tiles):
                        if L == 0:
                            v = vtok_e[:, kt, HD * (hh // 4):HD * (hh // 4) + HD]
                        else:
                            v = vtok_o[:, kt, HD * hh:HD * hh + HD]
                        ins = mm(o, v, pT[L][i % 3][:, n, :], n == 0, n == len(tiles) - 1)
                    if t >= 3:
                        ins.then_inc(psum_full, 1)

                if L == 0:
                    emptied(pe, "v ctx")
                else:
                    emptied(pe, ("v", 5))
                prepare(0)
                scores(0)
                for i, (hh, t) in enumerate(STEPS):
                    if i + 1 < len(STEPS):
                        if t == NT - 1:
                            prepare(hh + 1)
                        scores(i + 1)
                    if i >= 1:
                        values(i - 1)
                    turn(i)
                values(len(STEPS) - 1)

                pe.wait_ge(wout_in, 16 * (L + 1))
                emptied(pe, (L, "Oc", HEADS - 1))
                emptied(pe, ("u", "ctx") if L == 0 else ("gb", "ctx"))
                cat = [*(gated[:, k, :] for k in range(4)), *(oT[:, k, :] for k in range(4))] if L == 0 else \
                      [*(oT[:, k, :] for k in range(4)), *(yT[:, k, :] for k in range(4))]
                project((L, "out"), KD, w_out, 0, lambda k: cat[k], ctx_banks=2)

                norm_sums((L, "norm", 1), ones_d)
                pe.wait_ge(h_ready, KD * (2 * L + 2))
                pe.wait_ge(router_in, 16 * LAYERS)
                begin((L, "logits"))
                for t in range(NT):
                    for k in range(KD):
                        ins = mm(bank((L, "logits"))[:, E * t:E * t + E], hT[:, k, P * t:P * t + P], router[L][:, k, :], k == 0, k == KD - 1)
                ins.then_inc(psum_full, 1)
                pe.wait_ge(aff_done, L + 1)
                for name, tiles in (((L, "aff"), range(4)), ((L, "aff ctx"), [4])):
                    begin(name)
                    for j, t in enumerate(tiles):
                        ins = pe.transpose(bank(name)[0:E, P * j:P * j + P], aff[:, t, :], ident)
                    ins.then_inc(psum_full, 1)
                for t in range(NT):
                    begin((L, "h", t))
                    for k in range(KD):
                        ins = pe.transpose(pair((L, "h", t), n=D)[:, P * k:P * k + P], hT[:, k, P * t:P * t + P], ident)
                    ins.then_inc(psum_full, 1)
                pe.wait_ge(topk_done, L + 1)
                begin((L, "gates"))
                pe.transpose(bank((L, "gates"))[0:CAP, 0:E], vals, ident[0:E, 0:E])
                pe.transpose(bank((L, "gates"))[0:CAP, E:2 * E], idxf, ident[0:E, 0:E]).then_inc(psum_full, 1)
                emptied(pe, (L, "gates"))
                emptied(pe, (L, "h", NT - 1))
                emptied(pe, (L, "logits"))

                def turn_rows(s, arrived):
                    pe.wait_ge(gathered[s], arrived)
                    for k in range(KD):
                        ins = pe.transpose(psum[:, k // 4, CAP * (k % 4):CAP * (k % 4) + CAP], xs[s][:, P * k:P * k + P],
                                           ident[0:CAP, 0:CAP])
                    ins.then_inc(xsT_full, 1)

                def gate_up(s, done, arrived):
                    pe.wait_ge(xsT_ready, done)
                    for w, w_arrived, b in ((wg, wg_in, 2 + s), (wu, wu_in, 4 + s)):
                        pe.wait_ge(w_arrived[s], arrived)
                        for f in range(KF):
                            for k in range(KD):
                                ins = mm(psum[:, b, CAP * f:CAP * f + CAP], w[s][:, k, P * f:P * f + P], xsT[s][:, k, :],
                                         k == 0, k == KD - 1)
                    ins.then_inc(gu_full, 1)

                def down(s, done, arrived, evacuated=None):
                    pe.wait_ge(hid_ready, done)
                    pe.wait_ge(wd_in[s], arrived)
                    if evacuated is not None:
                        pe.wait_ge(y_ready, evacuated)
                    for half in range(2):
                        for f in range(KF):
                            ins = mm(psum[0:CAP, 6 + half, :], hid[s][:, f, :], wd[s][:, f, 512 * half:512 * half + 512],
                                     f == 0, f == KF - 1)
                    ins.then_inc(y_full, 1)

                n0, w0 = E * L, 16 * (E // 2) * L
                turn_rows(0, w0 + 16)
                gate_up(0, n0 + 1, w0 + 16)
                turn_rows(1, w0 + 16)
                gate_up(1, n0 + 2, w0 + 16)
                down(0, n0 + 1, w0 + 16)
                turn_rows(0, w0 + 32)
                gate_up(0, n0 + 3, w0 + 32)
                down(1, n0 + 2, w0 + 16, n0 + 1)
                with pe.Fori(1, E // 2 - 1) as i:
                    turn_rows(1, i * 16 + (w0 + 16))
                    gate_up(1, i * 2 + (n0 + 2), i * 16 + (w0 + 16))
                    down(0, i * 2 + (n0 + 1), i * 16 + (w0 + 16), i * 2 + n0)
                    turn_rows(0, i * 16 + (w0 + 32))
                    gate_up(0, i * 2 + (n0 + 3), i * 16 + (w0 + 32))
                    down(1, i * 2 + (n0 + 2), i * 16 + (w0 + 16), i * 2 + (n0 + 1))
                last = 16 * (E // 2)
                turn_rows(1, w0 + last)
                gate_up(1, n0 + E, w0 + last)
                down(0, n0 + E - 1, w0 + last, n0 + E - 2)
                down(1, n0 + E, w0 + last, n0 + E - 1)
                pe.wait_ge(y_ready, n0 + E)
                pe.wait_ge(acc_in, 16 * (L + 1))
                to_features((L, "moe"), xtok)

            norm_sums((LAYERS, "norm", 0), ones_d)
            pe.wait_ge(h_scaled, KD * (2 * LAYERS + 1))
            for t in range(NT):
                begin(("y", t))
                for k in range(KD):
                    ins = pe.transpose(pair(("y", t), n=D)[:, P * k:P * k + P], hT[:, k, P * t:P * t + P], ident)
                ins.then_inc(psum_full, 1)

        @block.scalar
        def _(act):
            used = [0]
            logs = [0]

            def freeing(ins):
                ins.then_inc(freed["act"], 1)

            def evacuate(name, dst, src, **kw):
                filled(act, name)
                freeing(nc.scalar.activation(dst, src, ACT.Copy, **kw))

            def squares(name, before, tiles):
                for k, src in enumerate(tiles):
                    if k >= 2:
                        act.wait_ge(sq_used, used[0] + k - 1)
                    elif k == 0 and before is not None:
                        filled(act, before)
                    nc.scalar.activation(sq[k % 2], src, ACT.Square).then_inc(sq_ready, 1)
                used[0] += len(tiles) - 1
                emptied(act, name)
                nc.scalar.activation(rstd, var, ACT.Ln).then_inc(log_done, 1)
                logs[0] += 1
                act.wait_ge(log_done, logs[0])
                nc.scalar.activation(rstd, rstd, ACT.Exp, scale=-0.5).then_inc(root_done, 1)

            def squares_of_x(L, which, before):
                emptied(act, x_last(L, which))
                squares((L, "norm", which), before, [xT[:, k, :] for k in range(KD)])

            def add_shift(L, which):
                for k in range(KD):
                    act.wait_ge(h_scaled, KD * (2 * L + which) + k + 1)
                    for g, grp in enumerate(GROUPS):
                        ins = nc.scalar.activation(hT[:, k, grp], hT[:, k, grp], ACT.Identity, bias=mod[:, L, 3 * which, k, g:g + 1])
                    ins.then_inc(h_ready, 1)

            filled(act, "cols")
            nc.scalar.activation(cols[:, 0:R_END], bank("cols")[:, 0:R_END], ACT.Copy).then_inc(freed["act"], 1)
            evacuate("bias cols", bcol[:, :], bank("bias cols")[:, 0:96])
            act.wait_ge(freed["act"], 2)
            for g, r in enumerate((R_C, R_CTX)):
                nc.scalar.activation(sT[:, :, g], cols[:, r:r + KD], ACT.Exp, scale=-1.0).then_inc(silu_exp, 1)
            for L in range(LAYERS):
                squares_of_x(L, 0, None if L == 0 else (L - 1, "norm", 1))
                add_shift(L, 0)
                if L == 0:
                    for j in range(2):
                        evacuate(f"wsT{j}", wsT[:, 4 * j:4 * j + 4, :].rearrange("p g q -> p (g q)"), bank(f"wsT{j}"))
                    for t in range(NT):
                        evacuate(("va", t), va[:, t, :], bank(("va", t)))
                    for m in range(4):
                        evacuate(("q", m), qT[:, m, LAT], bank(("q", m)))
                    evacuate(("q", "ctx"), qT[:, :, CTX], bank(("q", "ctx")).rearrange("p (m n) -> p m n", m=4))
                    evacuate(("k", 0), kT[:, P:P + NL], bank(("k", 0)))
                    evacuate(("k", "ctx"), kT[:, P + NL:KEYS], bank(("k", "ctx"))[:, 0:NC])
                    evacuate("v lat", vtok_e[:, 1:5, :].rearrange("p t n -> p (t n)"), bank("v lat"))
                    evacuate("v ctx", vtok_e[:, 5, :], bank("v ctx")[:, 0:P])
                    evacuate("cache k", kT[:, 0:P], bank("cache k")[:, 0:P])
                    emptied(act, "cache k")
                    for m in range(5):
                        squares(("qk norm", m), ("qk norm", m - 1) if m else (L, "norm", 0), [qT[:, m, :] if m < 4 else kT[:, P:KEYS]])
                    act.wait_ge(roped, 5)
                    for g in range(KV):
                        for half in range(2):
                            nc.scalar.activation(kdup[64 * half:64 * half + 64, g, :], kT[64 * g:64 * g + 64, :], ACT.Copy)\
                                .then_inc(kdup_ready, 1)
                else:
                    for m in range(4):
                        evacuate(("gc", m), zT[:, m, LAT], bank(("gc", m)))
                    evacuate(("gc", "ctx"), zT[:, :, CTX], bank(("gc", "ctx")).rearrange("p (m n) -> p m n", m=4))
                    for m in range(2):
                        evacuate(("cq", m), cq[:, m, LAT], bank(("cq", m)))
                    evacuate(("cq", "ctx"), cq[:, :, CTX], bank(("cq", "ctx"))[:, 0:2 * P].rearrange("p (m n) -> p m n", m=2))
                    evacuate(("ckv", 0), ckv[:, P:P + NL], bank(("ckv", 0)))
                    evacuate(("ckv", "ctx"), ckv[:, P + NL:KEYS], bank(("ckv", "ctx"))[:, 0:NC])
                    evacuate(("kr", 0), kr[:, P:P + NL], bank(("kr", 0))[64:96, :])
                    evacuate(("kr", "ctx"), kr[:, P + NL:KEYS], bank(("kr", "ctx"))[64:96, 0:NC])
                    evacuate("cache ckv", ckv[:, 0:P], bank("cache ckv")[:, 0:P])
                    evacuate("cache kr", kr[:, 0:P], bank("cache kr")[0:ROPE, 0:P])
                    emptied(act, "cache kr")
                    squares("cq norm", (L, "norm", 0), [cq[:, 0, :], cq[:, 1, :]])
                    squares("ckv norm", "cq norm", [ckv[:, P:KEYS]])
                    act.wait_ge(roped, 6)
                    for s in range(2):
                        nc.scalar.activation(kh[s][64:96, :], kr, ACT.Copy).then_inc(kr_copied, 1)
                    for t in range(KEYS // P):
                        evacuate(("v", t), vtok_o[:, t, :], bank(("v", t)))

                def prepare(hh):
                    if L == 0:
                        return
                    if hh % 2 == 0:
                        filled(act, ("kn", hh // 2))
                        src = pair(("kn", hh // 2), n=KEYS)
                        nc.scalar.activation(kh[0][0:64, :], src[0:64, :], ACT.Copy)
                        freeing(nc.scalar.activation(kh[1][0:64, :], src[64:128, :], ACT.Copy))
                    evacuate(("uq", hh), qh[hh % 2][0:QKC, :], pair(("uq", hh), QKC), scale=float(QKC) ** -0.5)

                def exponent(i):
                    n = len(STEPS) * L + i
                    width = P + NL if STEPS[i][1] < 4 else P
                    act.wait_ge(s_max, n + 1)
                    if i >= 2:
                        filled(act, (L, "T", i - 2))
                    act_ins = nc.scalar.activation(prob[i % 2][:, 0:width], pair((L, "S", i), n=width), ACT.Exp,
                                                   bias=stat[:, i % 2:i % 2 + 1], accum_out=stat[:, 2 + i % 2:3 + i % 2])
                    act_ins.then_inc(freed["act"], 1)

                def turned(i):
                    width = 5 if STEPS[i][1] < 4 else 1
                    evacuate((L, "T", i), pT[L][i % 3][:, 0:width, :].rearrange("p t n -> p (t n)"), pair((L, "T", i), n=P * width))

                prepare(0)
                exponent(0)
                for i, (hh, t) in enumerate(STEPS):
                    if i + 1 < len(STEPS):
                        if t == NT - 1:
                            prepare(hh + 1)
                        exponent(i + 1)
                    turned(i)

                squares_of_x(L, 1, (L, "T", len(STEPS) - 1))
                add_shift(L, 1)
                emptied(act, (L, "logits"))
                nc.scalar.activation(aff_e[:, :, :].rearrange("p t e -> p (t e)"), aff[:, :, :].rearrange("p t e -> p (t e)"),
                                     ACT.Exp).then_inc(aff_exp, 1)
                evacuate((L, "aff"), work[:, LAT], bank((L, "aff"))[0:E, :])
                evacuate((L, "aff ctx"), work[:, CTX], bank((L, "aff ctx"))[0:E, 0:NC])
                for t in range(NT):
                    if t >= 2:
                        act.wait_ge(h_out[t % 2], 16 * ((3 - t % 2) * L + t // 2))
                    evacuate((L, "h", t), htok[t % 2], pair((L, "h", t), n=D))
                filled(act, (L, "gates"))
                nc.scalar.activation(gates, bank((L, "gates"))[0:CAP, 0:E], ACT.Copy)
                freeing(nc.scalar.activation(slots, bank((L, "gates"))[0:CAP, E:2 * E], ACT.Copy))

                def rows_turned(s, e1):
                    act.wait_ge(xsT_full, e1)
                    nc.scalar.activation(xsT[s][:, :, :].rearrange("p (b k) n -> p b (k n)", b=2), psum[:, 0:2, 0:4 * CAP], ACT.Copy)\
                        .then_inc(xsT_ready, 1)

                def gate_exp(s, e1):
                    act.wait_ge(gu_full, e1)
                    nc.scalar.activation(sig[s][:, :, :].rearrange("p f n -> p (f n)"), psum[:, 2 + s, 0:KF * CAP], ACT.Exp, scale=-1.0)\
                        .then_inc(sig_exp, 1)

                n0 = E * L
                rows_turned(0, n0 + 1)
                gate_exp(0, n0 + 1)
                with act.Fori(0, E // 2 - 1) as i:
                    rows_turned(1, i * 2 + (n0 + 2))
                    gate_exp(1, i * 2 + (n0 + 2))
                    rows_turned(0, i * 2 + (n0 + 3))
                    gate_exp(0, i * 2 + (n0 + 3))
                rows_turned(1, n0 + E)
                gate_exp(1, n0 + E)
            squares_of_x(LAYERS, 0, (LAYERS - 1, "norm", 1))
            for t in range(NT):
                if t >= 2:
                    act.wait_ge(y_out[t % 2], 16 * (t // 2))
                evacuate(("y", t), ytok[t % 2], pair(("y", t), n=D))

        @block.vector
        def _(dve):
            step = [0]
            roots = [0]

            def then(ins):
                step[0] += 1
                ins.then_inc(dve_step, 1)
                dve.wait_ge(dve_step, step[0])

            def freeing(ins):
                ins.then_inc(freed["dve"], 1)

            def root_of(name):
                filled(dve, name)
                freeing(nc.vector.tensor_scalar(var, pair(name), EPS, None, ALU.add))
                roots[0] += 1
                dve.wait_ge(root_done, roots[0])
                then(nc.vector.tensor_tensor(var, var, rstd, ALU.mult))
                then(nc.vector.scalar_tensor_tensor(var, var, -0.5, rstd, ALU.mult, ALU.mult))
                then(nc.vector.scalar_tensor_tensor(rstd, var, 1.5, rstd, ALU.add, ALU.mult))

            def norm(L, which, name):
                root_of(name)
                for k in range(KD):
                    if L < LAYERS:
                        for g, grp in enumerate(GROUPS):
                            ins = nc.vector.scalar_tensor_tensor(hT[:, k, grp], xT[:, k, grp], amul[:, L, which, k, g:g + 1],
                                                                 rstd[:, grp], ALU.mult, ALU.mult)
                    else:
                        ins = nc.vector.scalar_tensor_tensor(hT[:, k, :], xT[:, k, :], cols[:, R_FIN + k:R_FIN + k + 1],
                                                             rstd, ALU.mult, ALU.mult)
                    ins.then_inc(h_scaled, 1)

            def add_to_x(kind, L, j):
                for k in range(KD):
                    filled(dve, (*kind, k) if kind[-1] == "moe" else (kind, k))
                    name = (*kind, k) if kind[-1] == "moe" else (kind, k)
                    freeing(nc.vector.scalar_tensor_tensor(xT[:, k, LAT], bank(name), mod[:, L, j, k, 0:1], xT[:, k, LAT],
                                                           ALU.mult, ALU.add))
                for b in range(2):
                    name = (*kind, f"ctx{b}") if kind[-1] == "moe" else (kind, f"ctx{b}")
                    filled(dve, name)
                    for m in range(4):
                        k = 4 * b + m
                        ins = nc.vector.scalar_tensor_tensor(xT[:, k, CTX], bank(name)[:, P * m:P * m + P], mod[:, L, j, k, 1:2],
                                                             xT[:, k, CTX], ALU.mult, ALU.add)
                    freeing(ins)

            dve.wait_ge(silu_exp, 2)
            then(nc.vector.tensor_scalar(sT_[:, :], sT_[:, :], 1.0, None, ALU.add))
            then(nc.vector.reciprocal(sT_[:, :], sT_[:, :]))
            for g, r in enumerate((R_C, R_CTX)):
                ins = nc.vector.tensor_tensor(sT[:, :, g], sT[:, :, g], cols[:, r:r + KD], ALU.mult)
            ins.then_inc(silu_ready, 1)
            for k in range(KD):
                filled(dve, ("x", k))
                freeing(nc.vector.tensor_copy(xT[:, k, LAT], bank(("x", k))))
            for b in range(2):
                filled(dve, ("x", f"ctx{b}"))
                freeing(nc.vector.tensor_copy(xT[:, 4 * b:4 * b + 4, CTX], bank(("x", f"ctx{b}")).rearrange("p (k n) -> p k n", k=4)))
            nb = MODC // P
            for c in range(LAYERS * 6 * D // MODC):
                filled(dve, ("mod", c))
                for g in range(2):
                    ins = nc.vector.tensor_tensor(mod_blocks[:, nb * c:nb * c + nb, g],
                                                  bank(("mod", c))[:, 0:2 * nb].rearrange("p (b g) -> p b g", g=2)[:, :, g],
                                                  bcol[:, nb * c:nb * c + nb], ALU.add)
                freeing(ins)
            emptied(dve, ("mod", LAYERS * 6 * D // MODC - 1))
            for L in range(LAYERS):
                for which, r in ((0, R_N1), (1, R_N2)):
                    for g in range(2):
                        ins = nc.vector.scalar_tensor_tensor(amul[:, L, which, :, g], mod[:, L, 1 + 3 * which, :, g], 1.0,
                                                             cols[:, r + KD * L:r + KD * L + KD], ALU.add, ALU.mult)
            then(ins)

            for L in range(LAYERS):
                norm(L, 0, (L, "norm", 0))
                if L == 0:
                    dve.wait_ge(zero_out, 16 * LAYERS * NT)
                    for g in range(4):
                        filled(dve, ("s", g))
                        freeing(nc.vector.tensor_copy(gated[:, g, LAT], bank(("s", g))))
                    filled(dve, ("s", "ctx"))
                    freeing(nc.vector.tensor_copy(gated[:, :, CTX], bank(("s", "ctx")).rearrange("p (m n) -> p m n", m=4)))
                    emptied(dve, ("s", "ctx"))
                    for m in range(4):
                        filled(dve, ("u", m))
                        freeing(nc.vector.tensor_tensor(gated[:, m, LAT], bank(("u", m)), gated[:, m, LAT], ALU.mult))
                    filled(dve, ("u", "ctx"))
                    freeing(nc.vector.tensor_tensor(gated[:, :, CTX], bank(("u", "ctx")).rearrange("p (m n) -> p m n", m=4),
                                                    gated[:, :, CTX], ALU.mult))
                    then(nc.vector.tensor_scalar(stat[:, 6:7], cols[:, R_EVQ:R_EVQ + 1], HD ** -0.5, None, ALU.mult))
                    dve.wait_ge(cs_in, 16)
                    for m in range(5):
                        name = ("qk norm", m)
                        root_of(name)
                        whole = qT[:, m, :] if m < 4 else kT[:, P:KEYS]
                        gain = stat[:, 6:7] if m < 4 else cols[:, R_EVK:R_EVK + 1]
                        nc.vector.scalar_tensor_tensor(whole, whole, gain, rstd, ALU.mult, ALU.mult).then_inc(proj_norm, 1)
                        filled(dve, ("qk rot", m))
                        x = whole[:, 0:NL]
                        freeing(nc.vector.tensor_tensor(tmp[0], bank(("qk rot", m)), rope_s, ALU.mult))
                        then(nc.vector.tensor_tensor(x, x, rope_c, ALU.mult))
                        nc.vector.tensor_tensor(x, x, tmp[0], ALU.add).then_inc(roped, 1)
                    filled(dve, "new k")
                    freeing(nc.vector.tensor_copy(small[:, P:2 * P], bank("new k")[:, 0:P]))
                else:
                    emptied(dve, ("gc", "ctx"))
                    for m in range(4):
                        filled(dve, ("hv", m))
                        freeing(nc.vector.tensor_tensor(zT[:, m, LAT], bank(("hv", m)), zT[:, m, LAT], ALU.mult))
                    filled(dve, ("hv", "ctx"))
                    freeing(nc.vector.tensor_tensor(zT[:, :, CTX], bank(("hv", "ctx")).rearrange("p (m n) -> p m n", m=4),
                                                    zT[:, :, CTX], ALU.mult))
                    emptied(dve, ("hv", "ctx"))
                    tap = lambda w, m: cols[:, R_CONV + 4 * w + m:R_CONV + 4 * w + m + 1]
                    for m in range(4):
                        ins = nc.vector.tensor_scalar(yT[:, m, :], zT[:, m, :], tap(1, m), None, ALU.mult)
                    then(ins)
                    for w, lo, zlo in ((0, 1, 0), (2, 0, 1)):
                        for m in range(4):
                            for base, n in ((0, NL), (NL, NC)):
                                y = yT[:, m, base + lo:base + lo + n - 1]
                                ins = nc.vector.scalar_tensor_tensor(y, zT[:, m, base + zlo:base + zlo + n - 1], tap(w, m), y,
                                                                     ALU.mult, ALU.add)
                        then(ins)
                    for m in range(4):
                        filled(dve, ("gb", m))
                        freeing(nc.vector.tensor_tensor(yT[:, m, LAT], bank(("gb", m)), yT[:, m, LAT], ALU.mult))
                    filled(dve, ("gb", "ctx"))
                    freeing(nc.vector.tensor_tensor(yT[:, :, CTX], bank(("gb", "ctx")).rearrange("p (m n) -> p m n", m=4),
                                                    yT[:, :, CTX], ALU.mult))
                    root_of("cq norm")
                    for m in range(2):
                        ins = nc.vector.scalar_tensor_tensor(cq[:, m, :], cq[:, m, :], cols[:, R_QA + m:R_QA + m + 1], rstd,
                                                             ALU.mult, ALU.mult)
                    ins.then_inc(proj_norm, 1)
                    dve.wait_ge(proj_norm, 6)
                    root_of("ckv norm")
                    nc.vector.scalar_tensor_tensor(ckv[:, P:KEYS], ckv[:, P:KEYS], cols[:, R_KVA:R_KVA + 1], rstd,
                                                   ALU.mult, ALU.mult).then_inc(proj_norm, 1)
                    dve.wait_ge(cs_in, 32)
                    filled(dve, "kr rot")
                    krl = kr[:, P:P + NL]
                    freeing(nc.vector.tensor_tensor(tmp[1][64:96, :], bank("kr rot")[64:96, :], rope_s[64:96, :], ALU.mult))
                    then(nc.vector.tensor_tensor(krl, krl, rope_c[64:96, :], ALU.mult))
                    nc.vector.tensor_tensor(krl, krl, tmp[1][64:96, :], ALU.add).then_inc(roped, 1)
                    for name, dst, w in (("new ckv", small[:, 160:160 + KVL], KVL), ("new kr", small[:, 288:288 + ROPE], ROPE)):
                        filled(dve, name)
                        freeing(nc.vector.tensor_copy(dst, bank(name)[:, 0:w]))

                def prepare(hh):
                    if L == 0:
                        return
                    name = ("uq rot", hh)
                    filled(dve, name)
                    x = qh[hh % 2][64:96, LAT]
                    freeing(nc.vector.tensor_tensor(tmp[1][64:96, :], bank(name)[64:96, :], rope_s[64:96, :], ALU.mult))
                    then(nc.vector.tensor_tensor(x, x, rope_c[64:96, :], ALU.mult))
                    nc.vector.tensor_tensor(x, x, tmp[1][64:96, :], ALU.add).then_inc(roped, 1)

                def maximum(i):
                    width = P + NL if STEPS[i][1] < 4 else P
                    filled(dve, (L, "S", i))
                    if i >= 2:
                        emptied(dve, (L, "S", i - 2))
                    nc.vector.tensor_reduce(stat[:, i % 2:i % 2 + 1], pair((L, "S", i), n=width), AX.X, ALU.max, negate=True)\
                        .then_inc(s_max, 1)

                def normalise(i):
                    width = P + NL if STEPS[i][1] < 4 else P
                    emptied(dve, (L, "S", i))
                    r = stat[:, 9 + i % 2:10 + i % 2]
                    then(nc.vector.reciprocal(r, stat[:, 2 + i % 2:3 + i % 2]))
                    nc.vector.tensor_scalar(prob[i % 2][:, 0:width], prob[i % 2][:, 0:width], r, None, ALU.mult).then_inc(s_norm, 1)

                def head_out(i):
                    hh, t = STEPS[i]
                    r = slice(64 * (hh % 2), 64 * (hh % 2) + 64)
                    if t == 3:
                        filled(dve, (L, "O", hh))
                        freeing(nc.vector.tensor_copy(oT[r, hh // 2, LAT], bank((L, "O", hh))[r, :]))
                    if t == 4:
                        filled(dve, (L, "Oc", hh))
                        freeing(nc.vector.tensor_copy(oT[r, hh // 2, CTX], bank((L, "Oc", hh))[r, 0:NC]))

                prepare(0)
                maximum(0)
                for i, (hh, t) in enumerate(STEPS):
                    normalise(i)
                    if i + 1 < len(STEPS):
                        if t == NT - 1:
                            prepare(hh + 1)
                        maximum(i + 1)
                    if i >= 1:
                        head_out(i - 1)
                head_out(len(STEPS) - 1)
                add_to_x((L, "out"), L, 2)

                norm(L, 1, (L, "norm", 1))
                name = (L, "logits")
                filled(dve, name)
                lg = bank(name)[:, 0:NT * E].rearrange("p (t e) -> p t e", t=NT)
                then(nc.vector.tensor_reduce(rowmax, lg, AX.X, ALU.max))
                ins = nc.vector.tensor_tensor(aff[:, :, :], lg, rowmax.rearrange("p (t o) -> p t o", o=1).to_broadcast([P, NT, E]), ALU.subtract)
                freeing(ins)
                dve.wait_ge(aff_exp, L + 1)
                then(nc.vector.tensor_reduce(rowsum, aff_e[:, :, :], AX.X, ALU.add))
                then(nc.vector.reciprocal(rowsum, rowsum))
                nc.vector.tensor_tensor(aff[:, :, :], aff_e[:, :, :], rowsum.rearrange("p (t o) -> p t o", o=1).to_broadcast([P, NT, E]), ALU.mult)\
                    .then_inc(aff_done, 1)
                emptied(dve, (L, "aff ctx"))
                for grp, at, cap in ((LAT, 0, CAP_L), (CTX, CAP_L, CAP_C)):
                    for r in range(cap // 8):
                        c8 = slice(at + 8 * r, at + 8 * r + 8)
                        then(nc.vector.max(vals[:, c8], work[:, grp]))
                        then(nc.vector.max_index(idx[:, c8], vals[:, c8], work[:, grp]))
                        then(nc.vector.match_replace(work[:, grp], vals[:, c8], work[:, grp], -1.0))
                then(nc.vector.tensor_copy(idxf, idx))
                nc.vector.tensor_scalar(idxf[:, CAP_L:CAP], idxf[:, CAP_L:CAP], float(NL), None, ALU.add).then_inc(topk_done, 1)

                def expert(s, e1, n4, used):
                    g, u = psum[:, 2 + s, 0:KF * CAP], psum[:, 4 + s, 0:KF * CAP]
                    x = sig[s][:, :, :].rearrange("p f n -> p (f n)")
                    dve.wait_ge(sig_exp, e1)
                    nc.vector.tensor_scalar(x, x, 1.0, None, ALU.add).then_inc(sig_step, 1)
                    dve.wait_ge(sig_step, n4 + 1)
                    nc.vector.reciprocal(x, x).then_inc(sig_step, 1)
                    dve.wait_ge(sig_step, n4 + 2)
                    nc.vector.tensor_tensor(x, g, x, ALU.mult).then_inc(sig_step, 1)
                    dve.wait_ge(sig_step, n4 + 3)
                    nc.vector.tensor_tensor(hid[s][:, :, :].rearrange("p f n -> p (f n)"), u, x, ALU.mult).then_inc(hid_ready, 1)

                def rows_out(s, e1, column, stored=None):
                    dve.wait_ge(y_full, e1)
                    if stored is not None:
                        dve.wait_ge(scattered, stored)
                    nc.vector.tensor_scalar(ysb[s].rearrange("p (b n) -> p b n", b=2), psum[0:CAP, 6:8, :], column, None, ALU.mult)\
                        .then_inc(y_ready, 1)

                n0 = E * L
                emptied(dve, (L, "gates"))
                expert(0, n0 + 1, 3 * n0, None)
                expert(1, n0 + 2, 3 * n0 + 3, None)
                rows_out(0, n0 + 1, gates[:, 0:1])
                expert(0, n0 + 3, 3 * n0 + 6, None)
                rows_out(1, n0 + 2, gates[:, 1:2])
                with dve.Fori(1, E // 2 - 1) as i:
                    expert(1, i * 2 + (n0 + 2), i * 6 + (3 * n0 + 3), None)
                    rows_out(0, i * 2 + (n0 + 1), gates[:, bass.ds(i * 2, 1)], i * 32 + 16 * (n0 - 1))
                    expert(0, i * 2 + (n0 + 3), i * 6 + (3 * n0 + 6), None)
                    rows_out(1, i * 2 + (n0 + 2), gates[:, bass.ds(i * 2 + 1, 1)], i * 32 + 16 * n0)
                expert(1, n0 + E, 3 * n0 + 3 * (E - 1), None)
                rows_out(0, n0 + E - 1, gates[:, E - 2:E - 1], 16 * (n0 + E - 3))
                rows_out(1, n0 + E, gates[:, E - 1:E], 16 * (n0 + E - 2))
                add_to_x((L, "moe"), L, 5)
            norm(LAYERS, 0, (LAYERS, "norm", 0))


_OUTS = {"y_prompt": (1, NC, D), "y_sample": (1, NL, D), "new_k": (1, 1, KV, NC, HD), "new_v": (1, 1, KV, NC, HD),
         "new_ckv": (1, 1, NC, KVL), "new_kr": (1, 1, NC, ROPE)}


def constants():
    c = np.zeros((P, C_END), np.float32)
    p = np.arange(P)
    c[p, C_ID + p] = 1.0
    c[:, C_ONED:C_ONED + P] = 1.0 / D
    c[:, C_BLK:C_BLK + P] = (p[:, None] // HD == p[None, :] // HD) / HD
    c[:, C_ONE2:C_ONE2 + P] = 1.0 / QL
    c[:, C_ONE1:C_ONE1 + P] = 1.0 / KVL
    for m in range(P):
        low = m % 32 < 16
        c[m + 16 if low else m - 16, C_PERM + m] = -1.0 if low else 1.0
    for m in range(ROPE):
        low = m % 16 < 8
        c[64 + (m + 8 if low else m - 8), C_PERMO + m] = -1.0 if low else 1.0
    for g in range(4):
        for m in range(P):
            c[2 * g + m // 64, C_SEL + P * g + m] = 1.0

    def table(rot, rows):
        axis = rot // 2
        inv = np.float32(10000.0) ** (-np.arange(0, axis, 2, dtype=np.float32) / np.float32(axis))
        t = np.arange(NL)
        pos = np.stack([t // GRID_W, t % GRID_W]).astype(np.float32)
        d = np.arange(rows) % rot
        ang = pos[d // axis] * inv[d % axis % (axis // 2)][:, None]
        return np.concatenate([np.cos(ang), np.sin(ang)], 1).astype(np.float32)

    return {"const": c, "rope_even": table(HD, P), "rope_odd": table(ROPE, ROPE)}


def kernel(**inputs):
    import concourse.bacc as _bacc
    from concourse.bass_utils import run_bass_kernel_spmd as _run

    nc = _bacc.Bacc("TRN2", target_bir_lowering=False, num_devices=1)
    arrays, args, outs = {}, {}, {}
    for name, value in {**inputs, **constants()}.items():
        v = np.ascontiguousarray(value)
        arrays[f"in_{name}"] = v
        args[name] = nc.dram_tensor(f"in_{name}", v.shape, mybir.dt.from_np(v.dtype), kind="ExternalInput").ap()
    for name, shape in _OUTS.items():
        outs[name] = nc.dram_tensor(f"out_{name}", shape, F32, kind="ExternalOutput").ap()
    trunk(nc, args, outs)
    r = _run(nc, [arrays], core_ids=[0])
    return tuple(r.results[0][f"out_{n}"] for n in _OUTS)
```

```python
from contextlib import ExitStack

import numpy as np

import concourse.bass as bass
from concourse import mybir

F32 = mybir.dt.float32
F32R = mybir.dt.float32r
U32 = mybir.dt.uint32
ALU = mybir.AluOpType
ACT = mybir.ActivationFunctionType
AX = mybir.AxisListType

P = 128
D = 1024
KD = D // P
NL, NC = 512, 128
T = NL + NC
HT = T // 2
NT = T // P
LAYERS = 2
HD = 64
HEADS, KV = 8, 2
GRID_W = 64
EPS = 1e-6
AW = 512
QL, KVL, ROPE, NOPE = 256, 128, 32, 64
QKC = NOPE + ROPE
KEYS = P + T
E = 16
CAP_L, CAP_C = 2 * NL // E, 2 * NC // E
CAP = CAP_L + CAP_C
FF = 512
KF = FF // P
MODC = 512
MODS = 6 * D // MODC
LAT, CTX = slice(0, NL), slice(NL, T)
GROUPS = (LAT, CTX)
PIECE = 2048
SLOTS, SPLITS = 4, 3

C_ID, C_ONED, C_BLK, C_ONE2, C_ONE1, C_PERM, C_PERMO, C_END = 0, 128, 256, 384, 512, 640, 768, 800

R_C, R_CTX, R_N1, R_N2, R_FIN, R_CONV, R_QA, R_KVA, R_EVQ, R_EVK, R_END = 0, 8, 16, 32, 48, 56, 68, 70, 71, 72, 73

STEPS = [(h, t) for h in range(HEADS) for t in range(NL // P)]
LATE = NL // P - 1
LKEYS = P + NL
PREPARE = (("uq rot", 1), ("kn", 1), ("vp", 1), ("uq", 2))
PREPARE_FIRST = (("uq", 0), ("uq rot", 0), ("kn", 0), ("vp", 0), ("uq", 1))

MOD_AT = {"start": [0, 1, 2, 3], ("qk", 0): [4], ("qk", 1): [5], ("qk", 2): [6], ("qk", 3): [7], ("qk", 4): [8, 9],
          (0, "norm"): [10], (0, "soft"): [11], (0, "top"): [12, 13, 14, 15, 16],
          "cq": [17, 18], "ckv": [19], "kr": [20, 21], (1, "norm"): [22], (1, "soft"): [], (1, "top"): [23]}

IN = {0: [("va", 512), ("va", 768), ("u", 0), ("u", 256), ("q", 1024), ("q", 1280), ("kv", 1536)],
      1: [("gc", 928), ("gc", 1184), ("hv", 1440), ("hv", 1696), ("gb", 416), ("gb", 672), ("cq", 0), ("ckv", 256)]}


class PsumPlan:

    def __init__(self):
        self.full, self.freed, self.reader, self.banks, self.order = {}, {}, {}, {}, []
        self.count = {"act": 0, "dve": 0}
        self.ring = 0

    def add(self, name, banks, reader, in_order=True):
        assert name not in self.full, name
        self.order.append(name)
        self.full[name] = len(self.order)
        self.reader[name], self.banks[name] = reader, banks
        if in_order:
            self.frees(name)

    def frees(self, name):
        self.count[self.reader[name]] += 1
        self.freed[name] = self.count[self.reader[name]]

    def one(self, name, reader, banks=1):
        b = self.ring % 8
        if banks == 2:
            b = (b + b % 2) % 8
        self.add(name, list(range(b, b + banks)), reader)
        self.ring = b + banks

    def before(self, name):
        at, found = self.full[name] - 1, []
        for b in self.banks[name]:
            for other in reversed(self.order[:at]):
                if b in self.banks[other]:
                    if other not in found:
                        found.append(other)
                    break
        return found


class Mods:

    def __init__(self):
        self.last = None

    def then(self, c):
        before, self.last = self.last, c
        return c, before

    def flush(self):
        before, self.last = self.last, None
        return before


def plan_psum():
    p = PsumPlan()
    one = p.one
    mods = Mods()

    def mod(at):
        for c in MOD_AT[at]:
            c, before = mods.then(c)
            one(("mod rows", c), "act")
            if before is not None:
                one(("mod turned", before), "dve")

    def flush():
        c = mods.flush()
        if c is not None:
            one(("mod turned", c), "dve")

    one("cols", "act"), one("bias cols", "act")
    for k in range(KD):
        one(("x", k), "dve")
    one(("x", "ctx0"), "dve"), one(("x", "ctx1"), "dve")
    one((0, "norm", 0), "dve", 2)
    mod("start"), flush()
    for L in range(LAYERS):
        if L > 0:
            one((L, "norm", 0), "dve", 2)
        if L == 0:
            one("wsT0", "act"), one("wsT1", "act")
            for j in range(2):
                for b in range(3):
                    one(("va", j, b), "act")
            for g in range(4):
                one(("s", g), "dve")
            one(("s", "ctx"), "dve")
            for m in range(4):
                one(("u", m), "dve", 2)
            for m in range(4):
                one(("q", m), "act", 2)
            one("k", "act", 2)
            one("v lat", "act"), one("v ctx", "act")
            one("cache k", "act")
            for m in range(5):
                one(("qk norm", m), "dve", 2)
                mod(("qk", m))
                one(("qk rot", m), "dve")
            flush()
            one("new k", "dve")
        else:
            for kind, reader in (("gc", "act"), ("hv", "dve"), ("gb", "dve")):
                for m in range(4):
                    one((kind, m), reader, 2)
            one(("cq", 0), "act", 2), one(("cq", 1), "act", 2)
            one("ckv", "act", 2), one("kr", "act", 2)
            one("cache ckv", "act"), one("cache kr", "act")
            one("cq norm", "dve", 2), mod("cq")
            one("ckv norm", "dve", 2), mod("ckv")
            one("kr rot", "dve"), mod("kr"), flush()
            one("new ckv", "dve"), one("new kr", "dve")

        def prepare(h, what):
            if L == 1 and h < HEADS:
                if what == "vp":
                    if h % 2 == 0:
                        p.add(("vp", h // 2), [4, 5], "act")
                elif what == "uq rot":
                    p.add(("uq rot", h), [4], "dve")
                else:
                    p.add((what, h), [4, 5], "act")

        for what, h in PREPARE_FIRST:
            prepare(h, what)
        for i in range(2):
            p.add((L, "S", i), [2 * i, 2 * i + 1], "act", in_order=False)
        p.frees((L, "S", 0))
        for i, (h, t) in enumerate(STEPS):
            if i + 1 < len(STEPS):
                p.frees((L, "S", i + 1))
            p.add((L, "T", i), [4, 5], "act")
            if i + 2 < len(STEPS):
                b = 2 * (i % 2)
                p.add((L, "S", i + 2), [b, b + 1], "act", in_order=False)
            what, ahead = PREPARE[t]
            prepare(h + ahead, what)
            if t == LATE:
                p.add((L, "O", h), [7], "dve")
                p.add((L, "Oc", h), [6], "dve")
        for m in range(KD):
            one((L, "out", m), "dve", 2)
        one((L, "norm", 1), "dve", 2)
        mod((L, "norm"))
        one((L, "logits"), "act", 2)
        one((L, "logits turned"), "dve")
        mod((L, "soft"))
        one((L, "aff"), "act"), one((L, "aff ctx"), "act")
        for t in range(NT):
            one((L, "h", t), "act", 2)
        mod((L, "top")), flush()
        one((L, "gates"), "act")
        for k in range(KD):
            one((L, "moe", k), "dve")
        one((L, "moe", "ctx0"), "dve"), one((L, "moe", "ctx1"), "dve")
    one((LAYERS, "norm", 0), "dve", 2)
    for t in range(NT):
        one(("y", t), "act", 2)
    return p


def plan_weights(a):
    stream = []

    def piece(key, src, split, used):
        n = 1
        for d in src.shape[1:]:
            n *= d
        q = sum(x["split"] for x in stream)
        stream.append(dict(key=key, src=src, split=split, used=used, p=len(stream), q=q if split else None, n=n, shape=src.shape[1:]))

    def rows(w):
        return w.rearrange("(k p) n -> p k n", p=P)

    def mod(at):
        for c in MOD_AT[at]:
            L, j = divmod(c, MODS)
            for half in range(2):
                piece(("mod", c, half), rows(a["w_mod"][L])[:, 4 * half:4 * half + 4, MODC * j:MODC * (j + 1)], False,
                      ("mod_used", c + 1) if half == 0 else ("mod rows", c))

    after = {"va": lambda m: ("va", m, 2), "kv": lambda m: "v ctx", "ckv": lambda m: "kr", "cq": lambda m: ("cq", 1)}
    mod("start")
    for L in range(LAYERS):
        seen = {}
        for kind, at in IN[L]:
            m = seen[kind] = seen.get(kind, -1) + 1
            width = 160 if kind == "ckv" else 256
            used = after[kind](m) if kind in after else (kind, 2 * m + 1)
            piece((kind, m), rows(a["ev_w_in" if L == 0 else "od_w_in"][0])[:, :, at:at + width], True, used)
        for at in ([("qk", m) for m in range(5)] if L == 0 else ["cq", "ckv", "kr"]):
            mod(at)
        for m in range(4):
            piece((L, "out", m), rows(a["ev_w_out" if L == 0 else "od_w_out"][0])[:, :, 256 * m:256 * m + 256], True, (L, "out", 2 * m + 1))
        mod((L, "norm")), mod((L, "soft")), mod((L, "top"))
        for m in range(6 * E):
            q = sum(x["split"] for x in stream)
            stream.append(dict(key=(L, "moe", m), split=True, used=("moe_used", 6 * E * L + m + 1), p=len(stream), q=q, n=PIECE))
    return stream, {x["key"]: x for x in stream}, {x["q"]: x for x in stream if x["split"]}


PIECES = {"g0": -2, "g1": -1, "u0": 0, "u1": 1, "d0": 8, "d1": 9}


def lin(e, mul, add):
    if isinstance(e, int):
        return mul * e + add
    i, off = e
    return i * (2 * mul) + (mul * off + add)


def plus(e, n):
    return e + n if isinstance(e, int) else (e[0], e[1] + n)


def first(e):
    return e if isinstance(e, int) else e[1]


def piece_number(e, what, add=0):
    if isinstance(e, int) and e == 0 and what[0] in "gu":
        return ("g0", "g1", "u0", "u1").index(what) + add
    if isinstance(e, int) and e == E - 1 and what[0] == "d":
        return 6 * E - 2 + int(what[1]) + add
    return lin(e, 6, PIECES[what] + add)



def trunk(nc, a, out):
    plan = plan_psum()
    stream, piece, split_piece = plan_weights(a)
    with ExitStack() as ctx:
        def sb(name, n, dt=F32, rows=P):
            return ctx.enter_context(nc.sbuf_tensor(name, [rows, n], dt))

        def sem(name):
            return ctx.enter_context(nc.semaphore(name))

        xT_ = sb("xT", KD * T)
        stage = sb("stage", SLOTS * PIECE)
        w_hi, w_lo = sb("w_hi", SPLITS * PIECE, F32R), sb("w_lo", SPLITS * PIECE, F32R)
        h_hi_, h_lo_ = sb("h_hi", KD * T, F32R), sb("h_lo", KD * T, F32R)
        ident_r = sb("ident_r", P, F32R)
        rt_hi, rt_lo = sb("router_hi", LAYERS * KD * E, F32R), sb("router_lo", LAYERS * KD * E, F32R)
        cst = sb("cst", C_END)
        cs = sb("cs", 2 * NL)
        cols = sb("cols", R_END + 1)
        bcol = sb("bcol", 96)
        sT_ = sb("sT", 2 * KD)
        mod_ = sb("mod", LAYERS * 48 * 2)
        amul_ = sb("amul", LAYERS * 2 * 2 * KD)
        mrow = sb("mrow", MODC)
        stat = sb("stat", 16)
        small = sb("small", 320)
        bs = small[0:8, P:2 * P]
        arena = sb("arena", 13568)
        psum = ctx.enter_context(nc.psum_tensor("psum", [P, 8, 512], F32))

        h_dram = [nc.dram_tensor(f"h_dram{L}", (T, D), F32).ap() for L in range(LAYERS)]
        acc_dram = [nc.dram_tensor(f"acc_dram{L}", (T, D), F32).ap() for L in range(LAYERS)]

        def v3(t, at, n, m):
            return t[:, at:at + n * m].rearrange("p (n m) -> p n m", n=n)

        xT = v3(xT_, 0, KD, T)
        h_hi, h_lo = v3(h_hi_, 0, KD, T), v3(h_lo_, 0, KD, T)
        ident, ones_d, blk64 = cst[:, C_ID:C_ID + P], cst[:, C_ONED:C_ONED + P], cst[:, C_BLK:C_BLK + P]
        ones_ql, ones_kvl = cst[:, C_ONE2:C_ONE2 + P], cst[:, C_ONE1:C_ONE1 + P]
        perm, permo = cst[:, C_PERM:C_PERM + P], cst[64:96, C_PERMO:C_PERMO + 32]
        sel = mrow[0:8, :].rearrange("p (g m) -> p g m", g=4)
        rope_c, rope_s = cs[:, 0:NL], cs[:, NL:2 * NL]
        sT = v3(sT_, 0, KD, 2)
        mod = mod_[:, :].rearrange("p (l j k g) -> p l j k g", l=LAYERS, j=6, k=KD)
        mod_blocks = mod_[:, :].rearrange("p (c g) -> p c g", g=2)
        amul = amul_[:, :].rearrange("p (l w k g) -> p l w k g", l=LAYERS, w=2, k=KD)
        sq = [arena[:, T * s:T * s + T] for s in range(2)]
        prob = hf = sq
        rstd = arena[:, 1280:1920]
        var = sq[1]
        qT = v3(arena, 1920, 4, T)
        kT = arena[:, 4480:4480 + KEYS]
        kpad = v3(arena, 9600, 2 * KV, KEYS)
        wsraw = v3(arena, 5248, 8, P)
        zeros = arena[:, 6272:6272 + D]
        vtok_e = v3(arena, 6784, 6, P)
        va = v3(arena, 7552, NT, AW)
        gated = v3(arena, 10112, 4, T)
        wsT = v3(arena, 12672, 7, P)
        wsT7 = sq[0][:, 0:P]
        tmp_e = arena[:, 12672:12672 + NL]

        def ws_tile(g):
            return wsT[:, g, :] if g < 7 else wsT7

        yT = v3(arena, 1920, 4, T)
        kh = [arena[:, 1920 + KEYS * s:1920 + KEYS * (s + 1)] for s in range(2)]
        w_uk, w_uv = arena[:, 3456:3968], arena[:, 3968:4480]
        zT = v3(arena, 4480, 4, T)
        cq = v3(arena, 7040, 2, T)
        ckv = arena[:, 8320:8320 + KEYS]
        kr = arena[64:96, 9088:9088 + KEYS]
        qh = [arena[:, 9856:9856 + T], rstd]
        vpair = [v3(arena, 10496 + KEYS * s, 6, P) for s in range(2)]
        w_uq = v3(arena, 12032, 2, HEADS * QKC)
        tmp_o = arena[:, 6400:6400 + NL]
        pT = {0: [v3(arena, 7552 + KEYS * s, NT + 1, P) for s in range(2)],
              1: [v3(arena, 4480 + KEYS * s, NT + 1, P) for s in range(2)]}
        prob_ctx = {0: arena[:, 9088:9216], 1: arena[:, 6016:6144]}
        tmp = {0: tmp_e, 1: tmp_o}
        htok = [arena[:, D * s:D * s + D] for s in range(2)]
        xs = [arena[0:CAP, 2048 + D * s:2048 + D * s + D] for s in range(2)]
        ysb = [arena[0:CAP, 4096 + D * s:4096 + D * s + D] for s in range(2)]
        aff, aff_e = v3(arena, 6144, NT, E), v3(arena, 6224, NT, E)
        lgT = arena[0:E, 6304:6304 + T]
        rowmax, rowsum = arena[:, 6944:6949], arena[:, 6949:6954]
        work = arena[0:E, 7584:7584 + T]
        sig, hid = arena[0:CAP, 8224:8224 + FF], arena[0:CAP, 8736:8736 + FF]
        vals = arena[0:E, 9248:9248 + CAP]
        idx = arena[0:E, 9328:9328 + CAP].bitcast(U32)
        idxf = arena[0:E, 9408:9408 + CAP]
        gates = arena[0:CAP, 9488:9488 + E]
        slots = arena[0:CAP, 9504:9504 + E].bitcast(U32)
        x_hi, x_lo = v3(h_hi_, 0, KD, CAP), v3(h_lo_, 0, KD, CAP)
        t_hi, t_lo = v3(h_hi_, 640, KF, CAP), v3(h_lo_, 640, KF, CAP)
        xtok = v3(arena, 7552, NT, D)
        final = v3(arena, 7552, KD, T)
        ytok = [arena[:, 2048 + D * s:2048 + D * s + D] for s in range(2)]

        consts_in, rows_in, x_in, router_in, sel_in, zeroed, zero_out = (
            sem(n) for n in ("consts_in", "rows_in", "x_in", "router_in", "sel_in", "zeroed", "zero_out"))
        psum_full = sem("psum_full")
        freed = {"act": sem("freed_act"), "dve": sem("freed_dve")}
        stage_in = [sem(f"stage_in{s}") for s in range(SLOTS)]
        hi_ready, lo_ready, mod_used, moe_used = (sem(n) for n in ("hi_ready", "lo_ready", "mod_used", "moe_used"))
        silu_ready, silu_exp = sem("silu_ready"), sem("silu_exp")
        cs_in, attn_w_in, cache_v_in, ukv_in = (sem(n) for n in ("cs_in", "attn_w_in", "cache_v_in", "ukv_in"))
        router_hi, router_lo = sem("router_hi_ready"), sem("router_lo_ready")
        log_done, root_done = sem("log_done"), sem("root_done")
        sq_ready, sq_used, h_scaled, h_hi_ready, h_lo_ready = (
            sem(n) for n in ("sq_ready", "sq_used", "h_scaled", "h_hi_ready", "h_lo_ready"))
        proj_norm = sem("proj_norm")
        roped = sem("roped")
        kpad_cleared, kpad_ready, kr_copied = sem("kpad_cleared"), sem("kpad_ready"), sem("kr_copied")
        cat_hi, cat_lo = sem("cat_hi"), sem("cat_lo")
        o_hi = sem("o_hi")
        new_out = sem("new_out")
        s_max, s_norm = sem("s_max"), sem("s_norm")
        aff_exp, aff_done, topk_done = (sem(n) for n in ("aff_exp", "aff_done", "topk_done"))
        h_out, y_out = [sem(f"h_out{s}") for s in range(2)], [sem(f"y_out{s}") for s in range(2)]
        gathered = [sem(f"gathered{s}") for s in range(2)]
        rows_full, rows_hi, rows_lo, silu_done, hid_ready, hidT_full, hidT_hi, hidT_lo, y_ready = (
            sem(n) for n in ("rows_full", "rows_hi", "rows_lo", "silu_done", "hid_ready", "hidT_full", "hidT_hi", "hidT_lo", "y_ready"))
        hid_step = sem("hid_step")
        scattered, acc_in = sem("scattered"), sem("acc_in")
        dve_step = sem("dve_step")

        def filled(eng, name):
            eng.wait_ge(psum_full, plan.full[name])

        def emptied(eng, name):
            eng.wait_ge(freed[plan.reader[name]], plan.freed[name])

        def bank(name, i=0):
            return psum[:, plan.banks[name][i], :]

        def pair(name, rows=P, n=T):
            b = plan.banks[name][0]
            return psum[0:rows, b:b + 2, :].rearrange("p b n -> p (b n)")[:, 0:n]

        def halves(name, rows=P):
            b = plan.banks[name][0]
            return psum[0:rows, b:b + 2, 0:HT]

        def two(t):
            return t.rearrange("p (b n) -> p b n", b=2)

        def group_halves(name):
            b = plan.banks[name][0]
            return ((psum[:, b, 0:HT], slice(0, HT), 0), (psum[:, b + 1, 0:NL - HT], slice(HT, NL), 0),
                    (psum[:, b + 1, NL - HT:HT], slice(NL, T), 1))

        def used(eng, pc):
            kind = pc["used"]
            if kind[0] == "moe_used":
                eng.wait_ge(moe_used, kind[1])
            elif kind[0] == "mod_used":
                eng.wait_ge(mod_used, kind[1])
            else:
                filled(eng, kind)

        def slot(pc):
            s = PIECE * (pc["p"] % SLOTS)
            return stage[:, s:s + pc["n"]]

        def split_slot(t, q, n=PIECE):
            return t[:, PIECE * (q % SPLITS):PIECE * (q % SPLITS) + n]

        def part(t, pc):
            return split_slot(t, pc["q"], pc["n"]).rearrange("p (k n) -> p k n", k=pc["shape"][0])

        def x_last(L, which, k):
            if L == 0 and which == 0:
                return ("x", "ctx1")
            return (L - 1, "moe", "ctx1") if which == 0 else (L - 1 + 1, "out", k)

        moe_p = [piece[(L, "moe", 0)]["p"] for L in range(LAYERS)]
        moe_q = [piece[(L, "moe", 0)]["q"] for L in range(LAYERS)]

        block = ctx.enter_context(nc.Block())

        @block.sync
        def _(sp):
            sp.dma_start(cst[:, :], a["const"]).then_inc(consts_in, 16)

            def row(at, src, n):
                sp.dma_start(small[at:at + n, 0:P], src).then_inc(rows_in, 16)

            row(R_C, a["c"].rearrange("b (k p) -> (b k) p", p=P), 8)
            row(R_CTX, a["c_ctx"].rearrange("(k p) -> k p", p=P), 8)
            row(R_N1, a["norm1"].rearrange("l (k p) -> (l k) p", p=P), 16)
            row(R_N2, a["norm2"].rearrange("l (k p) -> (l k) p", p=P), 16)
            row(R_FIN, a["final_norm"].rearrange("(k p) -> k p", p=P), 8)
            row(R_CONV, a["od_conv_w"].rearrange("l w (k p) -> (l w k) p", p=P), 12)
            row(R_QA, a["od_q_a_norm"].rearrange("l (k p) -> (l k) p", p=P), 2)
            row(R_KVA, a["od_kv_a_norm"], 1)
            for r, n in ((R_EVQ, "ev_q_norm"), (R_EVK, "ev_k_norm")):
                for half in range(2):
                    sp.dma_start(small[r:r + 1, HD * half:HD * half + HD], a[n]).then_inc(rows_in, 16)
            sp.dma_start(small[0:96, P:2 * P], a["b_mod"].rearrange("l (k p) -> (l k) p", p=P)).then_inc(rows_in, 16)

            def load(pc):
                if pc["p"] >= SLOTS:
                    before = stream[pc["p"] - SLOTS]
                    if before["split"]:
                        sp.wait_ge(lo_ready, before["q"] + 1)
                    else:
                        used(sp, before)
                sp.dma_start(slot(pc).rearrange("p (k n) -> p k n", k=pc["shape"][0]), pc["src"]).then_inc(stage_in[pc["p"] % SLOTS], 16)

            for L in range(LAYERS):
                start = 0 if L == 0 else moe_p[L - 1] + 6 * E
                for pc in stream[start:moe_p[L]]:
                    load(pc)
                wg, wu = (a[n][L].rearrange("e (k p) f -> e p k f", p=P) for n in ("moe_w_gate", "moe_w_up"))
                wd = a["moe_w_down"][L].rearrange("e (k p) n -> e p k n", p=P)

                def expert_piece(e, what):
                    m, m0, half = piece_number(e, what), piece_number(first(e), what), int(what[1])
                    if isinstance(e, int) and m < SLOTS:
                        before = stream[moe_p[L] + m - SLOTS]
                        if before["split"]:
                            sp.wait_ge(lo_ready, before["q"] + 1)
                        else:
                            used(sp, before)
                    else:
                        sp.wait_ge(lo_ready, m + (moe_q[L] - SLOTS + 1))
                    src = {"g": wg, "u": wu, "d": wd}[what[0]]
                    ee = slice(e, e + 1) if isinstance(e, int) else bass.ds(lin(e, 1, 0), 1)
                    if what[0] == "d":
                        src = src[ee, :, :, 512 * half:512 * half + 512]
                    else:
                        src = src[ee, :, 4 * half:4 * half + 4, :]
                    s = (moe_p[L] + m0) % SLOTS
                    sp.dma_start(stage[:, PIECE * s:PIECE * s + PIECE].rearrange("p (k n) -> p k n", k=4),
                                 src.rearrange("o p k n -> p (o k) n")).then_inc(stage_in[s], 16)

                for what in ("g0", "g1", "u0", "u1"):
                    expert_piece(0, what)

                def step(e):
                    for what in ("g0", "g1", "u0", "u1"):
                        expert_piece(plus(e, 1), what)
                    for what in ("d0", "d1"):
                        expert_piece(e, what)

                for e in range(3):
                    step(e)
                with sp.Fori(0, (E - 6) // 2) as i:
                    step((i, 3))
                    step((i, 4))
                step(E - 3)
                step(E - 2)
                expert_piece(E - 1, "d0")
                expert_piece(E - 1, "d1")

        @block.gpsimd
        def _(pool):
            for L in range(LAYERS):
                pool.dma_start(arena[:, 12672 + 128 * L:12800 + 128 * L].rearrange("p (k e) -> p k e", k=KD),
                               a["moe_router"][L].rearrange("(k p) e -> p k e", p=P)).then_inc(router_in, 16)
            pool.dma_start(wsraw, a["ev_w_s"][0].rearrange("g p q -> p g q")).then_inc(attn_w_in, 16)
            pool.dma_start(cs[:, :], a["rope_even"]).then_inc(cs_in, 16)
            pool.memset(zeros, 0.0).then_inc(zeroed, 1)
            filled(pool, "bias cols")
            pool.dma_start(bs, a["ev_b_s"][0]).then_inc(attn_w_in, 16)
            pool.dma_start(small[:, 0:P].rearrange("p (g d) -> p g d", g=KV),
                           a["cache_attn_k"][0, 0].rearrange("g s d -> s g d")).then_inc(attn_w_in, 16)
            filled(pool, ("mod turned", MOD_AT["start"][-1]))
            pool.dma_start(mrow[0:8, :], a["sel"]).then_inc(sel_in, 16)
            filled(pool, (0, "norm", 0))
            pool.wait_ge(zeroed, 1)
            for L in range(LAYERS):
                for t in range(NT):
                    pool.dma_start(acc_dram[L][P * t:P * t + P, :], zeros).then_inc(zero_out, 16)
            pool.wait_ge(zero_out, 16 * LAYERS * NT)
            pool.dma_start(vtok_e[:, 0, :].rearrange("p (g d) -> p g d", g=KV),
                           a["cache_attn_v"][0, 0].rearrange("g s d -> s g d")).then_inc(cache_v_in, 16)
            for L in range(LAYERS):
                if L == 0:
                    pool.wait_ge(cat_lo, 1)
                    pool.memset(kpad[:, :, :], 0.0).then_inc(kpad_cleared, 1)
                    emptied(pool, "v ctx")
                    pool.dma_start(out["new_v"][0, 0].rearrange("g s d -> s g d"),
                                   vtok_e[:, 5, :].rearrange("p (g d) -> p g d", g=KV)).then_inc(new_out, 16)
                    emptied(pool, "new k")
                    pool.dma_start(out["new_k"][0, 0].rearrange("g s d -> s g d"),
                                   small[:, P:2 * P].rearrange("p (g d) -> p g d", g=KV)).then_inc(new_out, 16)
                else:
                    pool.wait_ge(acc_in, 16)
                    emptied(pool, (0, "moe", "ctx1"))
                    pool.dma_start(cs[64:96, :], a["rope_odd"]).then_inc(cs_in, 16)
                    pool.wait_ge(new_out, 32)
                    pool.dma_start(small[:, 0:KVL], a["cache_mla_ckv"][0, 0]).then_inc(attn_w_in, 16)
                    pool.dma_start(small[:, KVL:KVL + ROPE], a["cache_mla_krope"][0, 0]).then_inc(attn_w_in, 16)
                    pool.dma_start(w_uq, a["od_w_uq"][0].rearrange("(k p) n -> p k n", p=P)).then_inc(attn_w_in, 16)
                    pool.wait_ge(cat_lo, 2)
                    ukv = a["od_w_ukv"][0].rearrange("r (h c) -> r h c", h=HEADS)
                    pool.dma_start(w_uk.rearrange("p (h c) -> p h c", h=HEADS), ukv[:, :, 0:NOPE]).then_inc(ukv_in, 16)
                    pool.dma_start(w_uv.rearrange("p (h c) -> p h c", h=HEADS), ukv[:, :, NOPE:NOPE + HD]).then_inc(ukv_in, 16)
                    emptied(pool, "new kr")
                    pool.dma_start(out["new_ckv"][0, 0], small[:, 160:160 + KVL]).then_inc(new_out, 16)
                    pool.dma_start(out["new_kr"][0, 0], small[:, 288:288 + ROPE]).then_inc(new_out, 16)
                emptied(pool, (L, "gates"))
                pool.wait_ge(h_out[0], 16 * 3 * (L + 1))
                pool.wait_ge(h_out[1], 16 * 2 * (L + 1))

                def gather(e):
                    if e >= 2:
                        pool.wait_ge(rows_full, E * L + e - 1)
                    pool.indirect_dma_start(xs[e % 2], None, h_dram[L], bass.IndirectOffsetOnAxis(slots[:, e:e + 1], 0))\
                        .then_inc(gathered[e % 2], 16)

                def scatter(e):
                    pool.wait_ge(y_ready, E * L + e + 1)
                    if e + L:
                        pool.wait_ge(scattered, 16 * (E * L + e))
                    pool.indirect_dma_start(acc_dram[L], bass.IndirectOffsetOnAxis(slots[:, e:e + 1], 0), ysb[e % 2], None,
                                            compute_op=ALU.add).then_inc(scattered, 16)

                gather(0)
                gather(1)
                for e in range(E):
                    if e + 2 < E:
                        gather(e + 2)
                    scatter(e)
            pool.wait_ge(new_out, 16 * 4)

        @block.tensor
        def _(pe):
            squared = [0]
            mods = Mods()

            def begin(name):
                for other in plan.before(name):
                    emptied(pe, other)

            def mm(o, w, x, first, last):
                return pe.matmul(o, w, x, start=first, stop=last, skip_group_check=True)

            def norm_sums(name, weights, tiles=KD):
                begin(name)
                for k in range(tiles):
                    squared[0] += 1
                    pe.wait_ge(sq_ready, squared[0])
                    mm(bank(name, 0), weights, sq[k % 2][:, LAT], k == 0, k == tiles - 1)
                    ins = mm(bank(name, 1)[:, 0:NC], weights, sq[k % 2][:, CTX], k == 0, k == tiles - 1)
                    ins.then_inc(sq_used if k < tiles - 1 else psum_full, 1)

            def to_features(kind, src):
                for k in range(KD):
                    begin((*kind, k))
                    for t in range(4):
                        ins = pe.transpose(bank((*kind, k))[:, P * t:P * t + P], src[:, t, P * k:P * k + P], ident)
                    ins.then_inc(psum_full, 1)
                for b in range(2):
                    name = (*kind, f"ctx{b}")
                    begin(name)
                    for j in range(4):
                        k = 4 * b + j
                        ins = pe.transpose(bank(name)[:, P * j:P * j + P], src[:, 4, P * k:P * k + P], ident)
                    ins.then_inc(psum_full, 1)

            def modulation(at):
                for c in MOD_AT[at]:
                    c, before = mods.then(c)
                    begin(("mod rows", c))
                    for half in range(2):
                        pc = piece[("mod", c, half)]
                        w = slot(pc).rearrange("p (k n) -> p k n", k=4)
                        pe.wait_ge(stage_in[pc["p"] % SLOTS], 16 * (pc["p"] // SLOTS + 1))
                        for k in range(4):
                            ins = mm(bank(("mod rows", c))[0:2, :], sT[:, 4 * half + k, :], w[:, k, :], half + k == 0, half == 1 and k == 3)
                        ins.then_inc(psum_full if half else mod_used, 1)
                    if before is not None:
                        turn_mod(before)

            def turn_mod(c):
                if c is None:
                    return
                emptied(pe, ("mod rows", c))
                begin(("mod turned", c))
                for b in range(MODC // P):
                    ins = pe.transpose(bank(("mod turned", c))[:, 2 * b:2 * b + 2], mrow[0:2, P * b:P * b + P], ident[0:2, 0:2])
                ins.then_inc(psum_full, 1)

            waited = [0]

            def h_tile(n):
                if n > waited[0]:
                    pe.wait_ge(h_hi_ready, n)
                    pe.wait_ge(h_lo_ready, n)
                    waited[0] = n

            def passes(o, w, x, first, last):
                mm(o, w[0], x[0], first, False)
                mm(o, w[0], x[1], False, False)
                return mm(o, w[1], x[0], False, last)

            def weights(key):
                pc = piece[key]
                pe.wait_ge(lo_ready, pc["q"] + 1)
                return part(w_hi, pc), part(w_lo, pc)

            def project(key, names, at=(0, P), h0=None):
                hi, lo = weights(key)
                for name, c in zip(names, at):
                    begin(name)
                    n = min(P, hi.shape[2] - c)
                    for k in range(KD):
                        if h0 is not None:
                            h_tile(h0 + k + 1)
                        w = (hi[:, k, c:c + n], lo[:, k, c:c + n])
                        for half in range(2):
                            tk = slice(HT * half, HT * half + HT)
                            ins = passes(bank(name, half)[0:n, 0:HT], w, (h_hi[:, k, tk], h_lo[:, k, tk]), k == 0, k == KD - 1)
                    ins.then_inc(psum_full, 1)

            pe.wait_ge(consts_in, 16)
            pe.wait_ge(rows_in, 16 * 13)
            pe.transpose(bank("cols")[:, 0:R_END], small[0:R_END, 0:P], ident[0:R_END, 0:R_END]).then_inc(psum_full, 1)
            pe.transpose(bank("bias cols")[:, 0:96], small[0:96, P:2 * P], ident[0:96, 0:96]).then_inc(psum_full, 1)
            pe.wait_ge(x_in, 32)
            to_features(("x",), xtok)
            norm_sums((0, "norm", 0), ones_d)
            pe.wait_ge(silu_ready, 1)
            modulation("start")
            turn_mod(mods.flush())

            for L in range(LAYERS):
                if L > 0:
                    norm_sums((L, "norm", 0), ones_d)
                h0 = 2 * KD * L
                if L == 0:
                    pe.wait_ge(attn_w_in, 16 * 3)
                    for j in range(2):
                        begin(f"wsT{j}")
                        for g in range(4):
                            ins = pe.transpose(bank(f"wsT{j}")[:, P * g:P * g + P], wsraw[:, 4 * j + g, :], ident)
                        ins.then_inc(psum_full, 1)
                    for j in range(2):
                        hi, lo = weights(("va", j))
                        for b, tiles in enumerate(((0, 1), (2, 3), (4,))):
                            name = ("va", j, b)
                            begin(name)
                            for n, t in enumerate(tiles):
                                for k in range(KD):
                                    h_tile(h0 + k + 1)
                                    tk = slice(P * t, P * t + P)
                                    ins = passes(bank(name)[:, 256 * n:256 * n + 256], (h_hi[:, k, tk], h_lo[:, k, tk]),
                                                 (hi[:, k, :], lo[:, k, :]), k == 0, k == KD - 1)
                            ins.then_inc(psum_full, 1)
                    emptied(pe, ("va", 1, 2))
                    emptied(pe, "wsT1")
                    pe.wait_ge(sel_in, 16)
                    for g in range(4):
                        begin(("s", g))
                        b_rows = bs.rearrange("p (o q) -> p o q", o=1).to_broadcast([8, 4, P])
                        mm(bank(("s", g)).rearrange("p (o q) -> p o q", o=4), sel[:, g, :], b_rows, True, False)
                        for t in range(4):
                            for j in range(2):
                                ins = mm(bank(("s", g))[64 * j:64 * j + 64, P * t:P * t + P],
                                         va[:, t, P * g + 64 * j:P * g + 64 * j + 64], ws_tile(2 * g + j), False, t == 3)
                        ins.then_inc(psum_full, 1)
                    begin(("s", "ctx"))
                    for g in range(4):
                        mm(bank(("s", "ctx"))[:, P * g:P * g + P], sel[:, g, :], bs, g == 0, False)
                        for j in range(2):
                            ins = mm(bank(("s", "ctx"))[64 * j:64 * j + 64, P * g:P * g + P],
                                     va[:, 4, P * g + 64 * j:P * g + 64 * j + 64], ws_tile(2 * g + j), False, g == 3)
                    ins.then_inc(psum_full, 1)
                    for kind in "uq":
                        for j in range(2):
                            project((kind, j), [(kind, 2 * j), (kind, 2 * j + 1)])
                    project(("kv", 0), ["k"])
                    hi, lo = weights(("kv", 0))
                    for name, tiles in (("v lat", range(4)), ("v ctx", [4])):
                        begin(name)
                        for j, t in enumerate(tiles):
                            for k in range(KD):
                                tk = slice(P * t, P * t + P)
                                ins = passes(bank(name)[:, P * j:P * j + P], (h_hi[:, k, tk], h_lo[:, k, tk]),
                                             (hi[:, k, P:2 * P], lo[:, k, P:2 * P]), k == 0, k == KD - 1)
                        ins.then_inc(psum_full, 1)
                    begin("cache k")
                    pe.transpose(bank("cache k")[:, 0:P], small[:, 0:P], ident).then_inc(psum_full, 1)
                    pe.wait_ge(cs_in, 16)
                    for m in range(5):
                        norm_sums(("qk norm", m), blk64, 1)
                        modulation(("qk", m))
                        pe.wait_ge(proj_norm, m + 1)
                        src = qT[:, m, LAT] if m < 4 else kT[:, P:P + NL]
                        begin(("qk rot", m))
                        mm(bank(("qk rot", m)), perm, src, True, True).then_inc(psum_full, 1)
                    turn_mod(mods.flush())
                    begin("new k")
                    pe.transpose(bank("new k")[:, 0:P], kT[:, P + NL:KEYS], ident).then_inc(psum_full, 1)
                    pe.wait_ge(kpad_ready, 4)
                    pe.wait_ge(roped, 5)
                else:
                    for kind in ("gc", "hv", "gb"):
                        for j in range(2):
                            project((kind, j), [(kind, 2 * j), (kind, 2 * j + 1)], h0=h0)
                    project(("cq", 0), [("cq", 0), ("cq", 1)])
                    project(("ckv", 0), ["ckv", "kr"])
                    pe.wait_ge(attn_w_in, 16 * 6)
                    begin("cache ckv")
                    pe.transpose(bank("cache ckv")[:, 0:P], small[:, 0:KVL], ident).then_inc(psum_full, 1)
                    begin("cache kr")
                    pe.transpose(bank("cache kr")[0:ROPE, 0:P], small[:, KVL:KVL + ROPE], ident).then_inc(psum_full, 1)
                    norm_sums("cq norm", ones_ql, 2)
                    modulation("cq")
                    norm_sums("ckv norm", ones_kvl, 1)
                    modulation("ckv")
                    pe.wait_ge(cs_in, 32)
                    emptied(pe, "kr")
                    begin("kr rot")
                    mm(bank("kr rot")[64:96, :], permo, kr[:, P:P + NL], True, True).then_inc(psum_full, 1)
                    modulation("kr")
                    turn_mod(mods.flush())
                    pe.wait_ge(proj_norm, 7)
                    begin("new ckv")
                    pe.transpose(bank("new ckv")[:, 0:P], ckv[:, P + NL:KEYS], ident).then_inc(psum_full, 1)
                    begin("new kr")
                    pe.transpose(bank("new kr")[:, 0:ROPE], kr[:, P + NL:KEYS], ident[64:96, 64:96]).then_inc(psum_full, 1)
                    pe.wait_ge(ukv_in, 32)
                    emptied(pe, "cache ckv")

                def prepare(hh, what):
                    if L == 0 or hh >= HEADS or (what == "vp" and hh % 2 == 1):
                        return
                    name = (what, hh // 2 if what == "vp" else hh)
                    if what == "uq rot":
                        emptied(pe, ("uq", hh))
                    begin(name)
                    if what == "kn":
                        own = slice(NOPE * hh, NOPE * hh + NOPE)
                        mm(bank(name, 0)[0:NOPE, :], w_uk[:, own], ckv[:, 0:512], True, True)
                        ins = mm(bank(name, 1)[0:NOPE, 0:KEYS - 512], w_uk[:, own], ckv[:, 512:KEYS], True, True)
                    elif what == "uq":
                        for b, grp, n in ((0, LAT, NL), (1, CTX, NC)):
                            for k in range(2):
                                ins = mm(bank(name, b)[0:QKC, 0:n], w_uq[:, k, QKC * hh:QKC * hh + QKC], cq[:, k, grp], k == 0, k == 1)
                    elif what == "uq rot":
                        ins = mm(bank(name)[64:96, :], permo, qh[hh % 2][64:96, LAT], True, True)
                    else:
                        for t in range(KEYS // P):
                            ins = mm(pair(name, n=KEYS)[:, P * t:P * t + P], ckv[:, P * t:P * t + P],
                                     w_uv[:, HD * hh:HD * hh + 2 * HD], True, True)
                    ins.then_inc(psum_full, 1)

                def scores(i):
                    hh, t = STEPS[i]
                    name = (L, "S", i)
                    begin(name)
                    q_at = P * t
                    if L == 0:
                        q, kk = qT[:, hh // 2, q_at:q_at + P], kpad[:, 2 * (hh // 4) + hh % 2, :]
                    else:
                        if t == 0:
                            pe.wait_ge(roped, 5 + 1 + hh + 1)
                            emptied(pe, ("kn", hh))
                            pe.wait_ge(kr_copied, 2)
                        q, kk = qh[hh % 2][0:QKC, q_at:q_at + P], kh[hh % 2][0:QKC, :]
                    mm(bank(name, 0), q, kk[:, 0:512], True, True)
                    ins = mm(bank(name, 1)[:, 0:P], q, kk[:, 512:LKEYS], True, True)
                    if t == LATE:
                        q = qT[:, hh // 2, CTX] if L == 0 else qh[hh % 2][0:QKC, CTX]
                        ins = mm(bank(name, 1)[:, P:2 * P], q, kk[:, LKEYS:KEYS], True, True)
                    ins.then_inc(psum_full, 1)

                def turn(i):
                    hh, t = STEPS[i]
                    name = (L, "T", i)
                    begin(name)
                    pe.wait_ge(s_norm, len(STEPS) * L + i + 1)
                    for kt in range(NT):
                        ins = pe.transpose(pair(name)[:, P * kt:P * kt + P], prob[i % 2][:, P * kt:P * kt + P], ident)
                    if t == LATE:
                        ins = pe.transpose(pair(name, n=KEYS)[:, LKEYS:KEYS], prob_ctx[L], ident)
                    ins.then_inc(psum_full, 1)

                def values(i):
                    hh, t = STEPS[i]
                    if t == 0:
                        begin((L, "O", hh))
                    emptied(pe, (L, "T", i))
                    r = slice(64 * (hh % 2), 64 * (hh % 2) + 64)

                    def v(kt):
                        if L == 0:
                            return vtok_e[:, kt, HD * (hh // 4):HD * (hh // 4) + HD]
                        return vpair[hh // 2 % 2][:, kt, HD * (hh % 2):HD * (hh % 2) + HD]

                    for kt in range(NT):
                        ins = mm(bank((L, "O", hh))[r, P * t:P * t + P], v(kt), pT[L][i % 2][:, kt, :], kt == 0, kt == NT - 1)
                    if t == LATE:
                        ins.then_inc(psum_full, 1)
                        begin((L, "Oc", hh))
                        mm(bank((L, "Oc", hh))[r, 0:P], v(NT), pT[L][i % 2][:, NT, :], True, True).then_inc(psum_full, 1)

                if L == 0:
                    emptied(pe, "v ctx")
                    pe.wait_ge(cache_v_in, 16)
                for what, hh in PREPARE_FIRST:
                    prepare(hh, what)
                scores(0)
                scores(1)
                for i, (hh, t) in enumerate(STEPS):
                    turn(i)
                    if i + 2 < len(STEPS):
                        scores(i + 2)
                    what, ahead = PREPARE[t]
                    prepare(hh + ahead, what)
                    values(i)

                pe.wait_ge(cat_lo, L + 1)
                emptied(pe, (L, "Oc", HEADS - 1))
                for j in range(4):
                    project((L, "out", j), [(L, "out", 2 * j), (L, "out", 2 * j + 1)])

                norm_sums((L, "norm", 1), ones_d)
                modulation((L, "norm"))
                name = (L, "logits")
                begin(name)
                pe.wait_ge(router_lo, 1)
                for k in range(KD):
                    h_tile(h0 + KD + k + 1)
                    c = slice(E * (KD * L + k), E * (KD * L + k) + E)
                    for half in range(2):
                        tk = slice(HT * half, HT * half + HT)
                        ins = passes(bank(name, half)[0:E, 0:HT], (rt_hi[:, c], rt_lo[:, c]), (h_hi[:, k, tk], h_lo[:, k, tk]),
                                     k == 0, k == KD - 1)
                ins.then_inc(psum_full, 1)
                emptied(pe, name)
                name = (L, "logits turned")
                begin(name)
                for t in range(NT):
                    ins = pe.transpose(bank(name)[:, E * t:E * t + E], lgT[:, P * t:P * t + P], ident[0:E, 0:E])
                ins.then_inc(psum_full, 1)
                modulation((L, "soft"))
                pe.wait_ge(aff_done, L + 1)
                for name, tiles in (((L, "aff"), range(4)), ((L, "aff ctx"), [4])):
                    begin(name)
                    for j, t in enumerate(tiles):
                        ins = pe.transpose(bank(name)[0:E, P * j:P * j + P], aff[:, t, :], ident)
                    ins.then_inc(psum_full, 1)
                for t in range(NT):
                    begin((L, "h", t))
                    for k in range(KD):
                        o = pair((L, "h", t), n=D)[:, P * k:P * k + P]
                        mm(o, h_hi[:, k, P * t:P * t + P], ident_r[:, :], True, False)
                        ins = mm(o, h_lo[:, k, P * t:P * t + P], ident_r[:, :], False, True)
                    ins.then_inc(psum_full, 1)
                modulation((L, "top"))
                turn_mod(mods.flush())
                pe.wait_ge(topk_done, L + 1)
                begin((L, "gates"))
                pe.transpose(bank((L, "gates"))[0:CAP, 0:E], vals, ident[0:E, 0:E])
                pe.transpose(bank((L, "gates"))[0:CAP, E:2 * E], idxf, ident[0:E, 0:E]).then_inc(psum_full, 1)
                emptied(pe, (L, "gates"))
                emptied(pe, (L, "h", NT - 1))
                emptied(pe, ("mod turned", MOD_AT[(L, "top")][-1]))
                n0 = E * L

                def turn_rows(e):
                    s = first(e) % 2
                    if isinstance(e, int):
                        pe.wait_ge(gathered[s], 16 * (8 * L + e // 2 + 1))
                    else:
                        pe.wait_ge(gathered[s], e[0] * 16 + 16 * (8 * L + e[1] // 2 + 1))
                    for k in range(KD):
                        ins = pe.transpose(psum[:, k // 4, CAP * (k % 4):CAP * (k % 4) + CAP], xs[s][:, P * k:P * k + P],
                                           ident[0:CAP, 0:CAP])
                    ins.then_inc(rows_full, 1)

                def expert_weights(e, what):
                    m = piece_number(e, what, moe_q[L] + 1)
                    pe.wait_ge(lo_ready, m)
                    q = moe_q[L] + piece_number(first(e), what)
                    return (split_slot(t, q).rearrange("p (k n) -> p k n", k=4) for t in (w_hi, w_lo))

                def rows_times(e, what, b):
                    hi, lo = expert_weights(e, what)
                    half = int(what[1])
                    for k in range(4):
                        kk = 4 * half + k
                        ins = passes(psum[0:CAP, b, :], (x_hi[:, kk, :], x_lo[:, kk, :]), (hi[:, k, :], lo[:, k, :]),
                                     kk == 0, kk == KD - 1)
                    ins.then_inc(moe_used, 1)

                def gate(e):
                    pe.wait_ge(rows_lo, lin(e, 1, n0 + 1))
                    pe.wait_ge(rows_hi, lin(e, 1, n0 + 1))
                    for what in ("g0", "g1"):
                        rows_times(e, what, 4 + first(e) % 2)

                def up(e):
                    for what in ("u0", "u1"):
                        rows_times(e, what, 3)

                def turn_hidden(e):
                    pe.wait_ge(hid_ready, lin(e, 1, n0 + 1))
                    for f in range(KF):
                        ins = pe.transpose(psum[:, 2, CAP * f:CAP * f + CAP], hid[:, P * f:P * f + P], ident[0:CAP, 0:CAP])
                    ins.then_inc(hidT_full, 1)

                def down(e):
                    pe.wait_ge(hidT_lo, lin(e, 1, n0 + 1))
                    pe.wait_ge(hidT_hi, lin(e, 1, n0 + 1))
                    if not (isinstance(e, int) and e == 0 and L == 0):
                        pe.wait_ge(y_ready, lin(e, 1, n0))
                    for half, what in enumerate(("d0", "d1")):
                        hi, lo = expert_weights(e, what)
                        for f in range(KF):
                            ins = passes(psum[0:CAP, 6 + half, :], (t_hi[:, f, :], t_lo[:, f, :]), (hi[:, f, :], lo[:, f, :]),
                                         f == 0, f == KF - 1)
                        ins.then_inc(moe_used, 1)

                def step(e, more=True):
                    gate(plus(e, 1))
                    turn_hidden(e)
                    up(plus(e, 1))
                    if more:
                        turn_rows(plus(e, 2))
                    down(e)

                turn_rows(0)
                gate(0)
                up(0)
                turn_rows(1)
                for e in range(3):
                    step(e)
                with pe.Fori(0, (E - 6) // 2) as i:
                    step((i, 3))
                    step((i, 4))
                step(E - 3)
                step(E - 2, False)
                turn_hidden(E - 1)
                down(E - 1)
                pe.wait_ge(y_ready, n0 + E)
                pe.wait_ge(acc_in, 16 * (L + 1))
                to_features((L, "moe"), xtok)

            norm_sums((LAYERS, "norm", 0), ones_d)
            pe.wait_ge(h_scaled, KD * (2 * LAYERS + 1))
            for t in range(NT):
                begin(("y", t))
                for k in range(KD):
                    ins = pe.transpose(pair(("y", t), n=D)[:, P * k:P * k + P], final[:, k, P * t:P * t + P], ident)
                ins.then_inc(psum_full, 1)

        @block.scalar
        def _(act):
            squares_used, logs = [0], [0]
            mods = Mods()

            def freeing(ins):
                ins.then_inc(freed["act"], 1)

            def evacuate(name, dst, src, **kw):
                filled(act, name)
                freeing(nc.scalar.activation(dst, src, ACT.Copy, **kw))

            def split(key):
                pc = piece[key]
                act.wait_ge(stage_in[pc["p"] % SLOTS], 16 * (pc["p"] // SLOTS + 1))
                if pc["q"] >= SPLITS:
                    used(act, split_piece[pc["q"] - SPLITS])
                nc.scalar.activation(split_slot(w_hi, pc["q"], pc["n"]), slot(pc), ACT.Copy).then_inc(hi_ready, 1)

            def squares(name, before, tiles, ready=None):
                for k, src in enumerate(tiles):
                    if k >= 2:
                        act.wait_ge(sq_used, squares_used[0] + k - 1)
                    elif k == 0 and before is not None:
                        filled(act, before)
                    if ready is not None:
                        emptied(act, ready(k))
                    nc.scalar.activation(sq[k % 2], src, ACT.Square).then_inc(sq_ready, 1)
                squares_used[0] += len(tiles) - 1
                emptied(act, name)
                nc.scalar.activation(rstd, var, ACT.Ln).then_inc(log_done, 1)
                logs[0] += 1
                act.wait_ge(log_done, logs[0])
                nc.scalar.activation(rstd, rstd, ACT.Exp, scale=-0.5).then_inc(root_done, 1)

            def squares_of_x(L, which, before):
                squares((L, "norm", which), before, [xT[:, k, :] for k in range(KD)], lambda k: x_last(L, which, k))

            def shifted(L, which):
                for k in range(KD):
                    act.wait_ge(h_scaled, KD * (2 * L + which) + k + 1)
                    for g, grp in enumerate(GROUPS):
                        ins = nc.scalar.activation(h_hi[:, k, grp], hf[k % 2][:, grp], ACT.Identity,
                                                   bias=mod[:, L, 3 * which, k, g:g + 1])
                    ins.then_inc(h_hi_ready, 1)

            def modulation(at):
                for c in MOD_AT[at]:
                    if c > 0:
                        filled(act, ("mod turned", c - 1))
                    evacuate(("mod rows", c), mrow[0:2, :], bank(("mod rows", c))[0:2, :])

            act.dma_start(xtok[:, 0:4, :], a["x_sample"].rearrange("b (t p) d -> p (b t) d", p=P)).then_inc(x_in, 16)
            act.dma_start(xtok[:, 4, :], a["x_prompt"][0]).then_inc(x_in, 16)
            evacuate("cols", cols[:, 0:R_END], bank("cols")[:, 0:R_END])
            evacuate("bias cols", bcol[:, :], bank("bias cols")[:, 0:96])
            emptied(act, "bias cols")
            for g, r in enumerate((R_C, R_CTX)):
                nc.scalar.activation(sT[:, :, g], cols[:, r:r + KD], ACT.Exp, scale=-1.0).then_inc(silu_exp, 1)
            act.wait_ge(router_in, 32)
            nc.scalar.activation(rt_hi[:, :], arena[:, 12672:12928], ACT.Copy).then_inc(router_hi, 1)
            squares_of_x(0, 0, None)
            modulation("start")
            mods.flush()
            for L in range(LAYERS):
                keys = [(kind, sum(k2 == kind for k2, _ in IN[L][:j])) for j, (kind, _) in enumerate(IN[L])]
                if L == 0:
                    for key in keys[:3]:
                        split(key)
                else:
                    squares_of_x(L, 0, (L - 1, "norm", 1))
                shifted(L, 0)
                if L == 0:
                    evacuate("wsT0", arena[:, 12672:12672 + 4 * P], bank("wsT0"))
                    filled(act, "wsT1")
                    act.wait_ge(h_lo_ready, KD)
                    nc.scalar.activation(arena[:, 12672 + 4 * P:12672 + 7 * P], bank("wsT1")[:, 0:3 * P], ACT.Copy)
                    freeing(nc.scalar.activation(wsT7, bank("wsT1")[:, 3 * P:4 * P], ACT.Copy))
                    for j in range(2):
                        for b, (t0, n) in enumerate(((0, 2), (2, 2), (4, 1))):
                            evacuate(("va", j, b), va[:, t0:t0 + n, 256 * j:256 * j + 256],
                                     bank(("va", j, b))[:, 0:256 * n].rearrange("p (t n) -> p t n", t=n))
                        split(keys[3 + j])
                    split(keys[5])
                    split(keys[6])
                    for j in range(2):
                        for m in (2 * j, 2 * j + 1):
                            evacuate(("q", m), two(qT[:, m, :]), halves(("q", m)))
                    evacuate("k", two(kT[:, P:KEYS]), halves("k"))
                    act.wait_ge(zero_out, 16 * LAYERS * NT)
                    evacuate("v lat", vtok_e[:, 1:5, :].rearrange("p t n -> p (t n)"), bank("v lat"))
                    evacuate("v ctx", vtok_e[:, 5, :], bank("v ctx")[:, 0:P])
                    evacuate("cache k", kT[:, 0:P], bank("cache k")[:, 0:P])
                    emptied(act, ("u", 3))
                    nc.scalar.activation(h_hi_[:, 0:4 * T], gated[:, :, :].rearrange("p m n -> p (m n)"), ACT.Copy).then_inc(cat_hi, 1)
                    emptied(act, "cache k")
                    for m in range(5):
                        squares(("qk norm", m), ("qk norm", m - 1) if m else (L, "norm", 0), [qT[:, m, :] if m < 4 else kT[:, P:KEYS]])
                        modulation(("qk", m))
                    mods.flush()
                    act.wait_ge(roped, 5)
                    act.wait_ge(kpad_cleared, 1)
                    for g in range(KV):
                        for half in range(2):
                            nc.scalar.activation(kpad[64 * half:64 * half + 64, 2 * g + half, :], kT[64 * g:64 * g + 64, :], ACT.Copy)\
                                .then_inc(kpad_ready, 1)
                else:
                    for j in range(2):
                        for m in (2 * j, 2 * j + 1):
                            evacuate(("gc", m), two(zT[:, m, :]), halves(("gc", m)))
                        split(keys[3 + j])
                    for key in keys[5:8]:
                        split(key)
                    for m in range(2):
                        evacuate(("cq", m), two(cq[:, m, :]), halves(("cq", m)))
                    evacuate("ckv", two(ckv[:, P:KEYS]), halves("ckv"))
                    evacuate("kr", two(kr[:, P:KEYS]), halves("kr", ROPE))
                    evacuate("cache ckv", ckv[:, 0:P], bank("cache ckv")[:, 0:P])
                    evacuate("cache kr", kr[:, 0:P], bank("cache kr")[0:ROPE, 0:P])
                    emptied(act, ("gb", 3))
                    nc.scalar.activation(h_hi_[:, 4 * T:8 * T], yT[:, :, :].rearrange("p m n -> p (m n)"), ACT.Copy).then_inc(cat_hi, 1)
                    emptied(act, "cache kr")
                    squares("cq norm", (L, "norm", 0), [cq[:, 0, :], cq[:, 1, :]])
                    modulation("cq")
                    squares("ckv norm", "cq norm", [ckv[:, P:KEYS]])
                    modulation("ckv")
                    modulation("kr")
                    mods.flush()
                    act.wait_ge(roped, 6)
                    act.wait_ge(cat_lo, 2)
                    for s in range(2):
                        nc.scalar.activation(kh[s][64:96, :], kr, ACT.Copy).then_inc(kr_copied, 1)

                def prepare(hh, what):
                    if L == 0 or hh >= HEADS:
                        return
                    if what == "kn":
                        evacuate(("kn", hh), kh[hh % 2][0:NOPE, :], pair(("kn", hh), NOPE, KEYS))
                    if what == "uq":
                        evacuate(("uq", hh), qh[hh % 2][0:QKC, :], pair(("uq", hh), QKC), scale=float(QKC) ** -0.5)
                    if what == "vp" and hh % 2 == 0:
                        evacuate(("vp", hh // 2), vpair[hh // 2 % 2][:, :, :].rearrange("p t n -> p (t n)"), pair(("vp", hh // 2), n=KEYS))

                def exponent(i):
                    act.wait_ge(s_max, len(STEPS) * L + i + 1)
                    if i >= 2:
                        filled(act, (L, "T", i - 2))
                    src = pair((L, "S", i), n=KEYS)
                    ins = nc.scalar.activation(prob[i % 2], src[:, 0:LKEYS], ACT.Exp, bias=stat[:, i % 2:i % 2 + 1],
                                               accum_out=stat[:, 2 + i % 2:3 + i % 2])
                    if STEPS[i][1] == LATE:
                        ins = nc.scalar.activation(prob_ctx[L], src[:, LKEYS:KEYS], ACT.Exp, bias=stat[:, 11:12],
                                                   accum_out=stat[:, 12:13])
                    freeing(ins)

                def turned(i):
                    width = KEYS if STEPS[i][1] == LATE else LKEYS
                    evacuate((L, "T", i), pT[L][i % 2][:, 0:width // P, :].rearrange("p t n -> p (t n)"), pair((L, "T", i), n=width))

                def head_out(i):
                    hh, t = STEPS[i]
                    if t < LATE:
                        return
                    r = slice(64 * (hh % 2), 64 * (hh % 2) + 64)
                    kk = (4 if L == 0 else 0) + hh // 2
                    filled(act, (L, "O", hh))
                    nc.scalar.activation(h_hi[r, kk, LAT], bank((L, "O", hh))[r, :], ACT.Copy).then_inc(o_hi, 1)
                    filled(act, (L, "Oc", hh))
                    nc.scalar.activation(h_hi[r, kk, CTX], bank((L, "Oc", hh))[r, 0:NC], ACT.Copy).then_inc(o_hi, 1)

                for what, hh in PREPARE_FIRST:
                    prepare(hh, what)
                exponent(0)
                for i, (hh, t) in enumerate(STEPS):
                    if i + 1 < len(STEPS):
                        exponent(i + 1)
                    if i >= 1:
                        head_out(i - 1)
                    turned(i)
                    what, ahead = PREPARE[t]
                    prepare(hh + ahead, what)
                    if i in (8, 16, 24):
                        split((L, "out", i // 8 - 1))
                head_out(len(STEPS) - 1)
                split((L, "out", 3))

                squares_of_x(L, 1, (L, "T", len(STEPS) - 1))
                shifted(L, 1)
                modulation((L, "norm"))
                evacuate((L, "logits"), two(lgT), halves((L, "logits"), E))
                emptied(act, (L, "logits turned"))
                nc.scalar.activation(aff_e[:, :, :].rearrange("p t e -> p (t e)"), aff[:, :, :].rearrange("p t e -> p (t e)"),
                                     ACT.Exp).then_inc(aff_exp, 1)
                modulation((L, "soft"))
                evacuate((L, "aff"), work[:, LAT], bank((L, "aff"))[0:E, :])
                evacuate((L, "aff ctx"), work[:, CTX], bank((L, "aff ctx"))[0:E, 0:NC])
                for t in range(NT):
                    if t >= 2:
                        act.wait_ge(h_out[t % 2], 16 * ((3 - t % 2) * L + t // 2))
                    evacuate((L, "h", t), htok[t % 2], pair((L, "h", t), n=D))
                    emptied(act, (L, "h", t))
                    act.dma_start(h_dram[L][P * t:P * t + P, :], htok[t % 2]).then_inc(h_out[t % 2], 16)
                modulation((L, "top"))
                mods.flush()
                filled(act, (L, "gates"))
                nc.scalar.activation(gates, bank((L, "gates"))[0:CAP, 0:E], ACT.Copy)
                freeing(nc.scalar.activation(slots, bank((L, "gates"))[0:CAP, E:2 * E], ACT.Copy))

                n0 = E * L

                def expert_split(e, what):
                    m, m0 = piece_number(e, what), piece_number(first(e), what)
                    p0, q0 = moe_p[L] + m0, moe_q[L] + m0
                    if isinstance(e, int):
                        act.wait_ge(stage_in[p0 % SLOTS], 16 * (p0 // SLOTS + 1))
                        used(act, split_piece[q0 - SPLITS])
                    else:
                        act.wait_ge(stage_in[p0 % SLOTS], e[0] * (16 * 12 // SLOTS) + 16 * (p0 // SLOTS + 1))
                        act.wait_ge(moe_used, m + (6 * n0 - SPLITS + 1))
                    nc.scalar.activation(split_slot(w_hi, q0), stage[:, PIECE * (p0 % SLOTS):PIECE * (p0 % SLOTS) + PIECE], ACT.Copy)\
                        .then_inc(hi_ready, 1)

                def rows_split(e):
                    act.wait_ge(rows_full, lin(e, 1, n0 + 1))
                    nc.scalar.activation(x_hi.rearrange("p (b k) n -> p b (k n)", b=2), psum[:, 0:2, 0:4 * CAP], ACT.Copy)\
                        .then_inc(rows_hi, 1)

                def hidden_split(e):
                    act.wait_ge(hidT_full, lin(e, 1, n0 + 1))
                    nc.scalar.activation(t_hi.rearrange("p f n -> p (f n)"), psum[:, 2, 0:KF * CAP], ACT.Copy).then_inc(hidT_hi, 1)

                def gate_silu(e):
                    act.wait_ge(moe_used, piece_number(e, "u1", 6 * n0 + 1))
                    nc.scalar.activation(sig, psum[0:CAP, 4 + first(e) % 2, :], ACT.Silu).then_inc(silu_done, 1)

                def rows_out(e):
                    act.wait_ge(moe_used, piece_number(e, "d1", 6 * n0 + 1))
                    if not (isinstance(e, int) and e < 2):
                        act.wait_ge(scattered, lin(e, 16, 16 * (n0 - 1)))
                    col = gates[:, e:e + 1] if isinstance(e, int) else gates[:, bass.ds(lin(e, 1, 0), 1)]
                    s = first(e) % 2
                    nc.scalar.activation(ysb[s].rearrange("p (b n) -> p b n", b=2), psum[0:CAP, 6:8, :], ACT.Copy, scale=col)\
                        .then_inc(y_ready, 1)

                def step(e, more=True):
                    expert_split(plus(e, 1), "u0")
                    if not (isinstance(e, int) and e == 0):
                        rows_out(plus(e, -1))
                    expert_split(plus(e, 1), "u1")
                    hidden_split(e)
                    expert_split(e, "d0")
                    expert_split(e, "d1")
                    if more:
                        rows_split(plus(e, 2))
                    gate_silu(plus(e, 1))
                    if more:
                        expert_split(plus(e, 2), "g0")
                        expert_split(plus(e, 2), "g1")

                for what in ("g0", "g1", "u0"):
                    expert_split(0, what)
                rows_split(0)
                expert_split(0, "u1")
                expert_split(1, "g0")
                expert_split(1, "g1")
                rows_split(1)
                gate_silu(0)
                for e in range(3):
                    step(e)
                with act.Fori(0, (E - 6) // 2) as i:
                    step((i, 3))
                    step((i, 4))
                step(E - 3)
                step(E - 2, False)
                expert_split(E - 1, "d0")
                rows_out(E - 2)
                hidden_split(E - 1)
                expert_split(E - 1, "d1")
                rows_out(E - 1)
                if L + 1 < LAYERS:
                    for key in [(kind, sum(k2 == kind for k2, _ in IN[L + 1][:j])) for j, (kind, _) in enumerate(IN[L + 1])][:3]:
                        split(key)
                act.wait_ge(scattered, 16 * E * (L + 1))
                act.dma_start(xtok, acc_dram[L].rearrange("(t p) d -> p t d", p=P)).then_inc(acc_in, 16)
            squares_of_x(LAYERS, 0, (LAYERS - 1, "norm", 1))
            for t in range(NT):
                if t >= 2:
                    act.wait_ge(y_out[t % 2], 16 * (t // 2))
                evacuate(("y", t), ytok[t % 2], pair(("y", t), n=D))
                emptied(act, ("y", t))
                dst = out["y_sample"][0, P * t:P * t + P, :] if t < NT - 1 else out["y_prompt"][0]
                act.dma_start(dst, ytok[t % 2]).then_inc(y_out[t % 2], 16)
            act.wait_ge(y_out[0], 16 * 3)
            act.wait_ge(y_out[1], 16 * 2)

        @block.vector
        def _(dve):
            step_count, roots = [0], [0]
            mods = Mods()

            def then(ins):
                step_count[0] += 1
                ins.then_inc(dve_step, 1)
                dve.wait_ge(dve_step, step_count[0])

            def freeing(ins):
                ins.then_inc(freed["dve"], 1)

            def rest(dst, src, hi):
                return nc.vector.tensor_tensor(dst, src, hi.bitcast(F32), ALU.subtract)

            def split(key):
                pc = piece[key]
                dve.wait_ge(hi_ready, pc["q"] + 1)
                rest(split_slot(w_lo, pc["q"], pc["n"]), slot(pc), split_slot(w_hi, pc["q"], pc["n"])).then_inc(lo_ready, 1)

            def root_of(name):
                filled(dve, name)
                freeing(nc.vector.tensor_scalar(var, pair(name), EPS, None, ALU.add))
                roots[0] += 1
                dve.wait_ge(root_done, roots[0])
                then(nc.vector.tensor_tensor(var, var, rstd, ALU.mult))
                then(nc.vector.scalar_tensor_tensor(var, var, -0.5, rstd, ALU.mult, ALU.mult))
                then(nc.vector.scalar_tensor_tensor(rstd, var, 1.5, rstd, ALU.add, ALU.mult))

            def norm(L, which):
                if (L, which) != (0, 0):
                    root_of((L, "norm", which))
                if L == LAYERS:
                    for k in range(KD):
                        nc.vector.scalar_tensor_tensor(final[:, k, :], xT[:, k, :], cols[:, R_FIN + k:R_FIN + k + 1], rstd,
                                                       ALU.mult, ALU.mult).then_inc(h_scaled, 1)
                    return
                for k in range(KD + 1):
                    if k < KD:
                        for g, grp in enumerate(GROUPS):
                            ins = nc.vector.scalar_tensor_tensor(hf[k % 2][:, grp], xT[:, k, grp], amul[:, L, which, k, g:g + 1],
                                                                 rstd[:, grp], ALU.mult, ALU.mult)
                        ins.then_inc(h_scaled, 1)
                    if k >= 1:
                        j = k - 1
                        dve.wait_ge(h_hi_ready, KD * (2 * L + which) + j + 1)
                        for g, grp in enumerate(GROUPS):
                            ins = nc.vector.scalar_tensor_tensor(h_lo[:, j, grp], hf[j % 2][:, grp], mod[:, L, 3 * which, j, g:g + 1],
                                                                 h_hi[:, j, grp].bitcast(F32), ALU.add, ALU.subtract)
                        ins.then_inc(h_lo_ready, 1)
                        if j < KD - 1:
                            dve.wait_ge(h_lo_ready, KD * (2 * L + which) + j + 1)

            def add_to_x(L, names, j):
                for k in range(KD):
                    name = (*names, k)
                    filled(dve, name)
                    freeing(nc.vector.scalar_tensor_tensor(xT[:, k, LAT], bank(name), mod[:, L, j, k, 0:1], xT[:, k, LAT],
                                                           ALU.mult, ALU.add))
                for b in range(2):
                    name = (*names, f"ctx{b}")
                    filled(dve, name)
                    for m in range(4):
                        k = 4 * b + m
                        ins = nc.vector.scalar_tensor_tensor(xT[:, k, CTX], bank(name)[:, P * m:P * m + P], mod[:, L, j, k, 1:2],
                                                             xT[:, k, CTX], ALU.mult, ALU.add)
                    freeing(ins)

            def turned_mod(c):
                if c is None:
                    return
                nb = MODC // P
                filled(dve, ("mod turned", c))
                for g in range(2):
                    ins = nc.vector.tensor_tensor(mod_blocks[:, nb * c:nb * c + nb, g],
                                                  bank(("mod turned", c))[:, 0:2 * nb].rearrange("p (b g) -> p b g", g=2)[:, :, g],
                                                  bcol[:, nb * c:nb * c + nb], ALU.add)
                freeing(ins)
                L, j = divmod(c, MODS)
                if j in (3, 9):
                    emptied(dve, ("mod turned", c))
                    which, r = (0, R_N1) if j == 3 else (1, R_N2)
                    for g in range(2):
                        ins = nc.vector.scalar_tensor_tensor(amul[:, L, which, :, g], mod[:, L, 1 + 3 * which, :, g], 1.0,
                                                             cols[:, r + KD * L:r + KD * L + KD], ALU.add, ALU.mult)
                    then(ins)

            def modulation(at):
                for c in MOD_AT[at]:
                    turned_mod(mods.then(c)[1])

            dve.wait_ge(silu_exp, 2)
            then(nc.vector.tensor_scalar(sT_[:, :], sT_[:, :], 1.0, None, ALU.add))
            then(nc.vector.reciprocal(sT_[:, :], sT_[:, :]))
            for g, r in enumerate((R_C, R_CTX)):
                ins = nc.vector.tensor_tensor(sT[:, :, g], sT[:, :, g], cols[:, r:r + KD], ALU.mult)
            ins.then_inc(silu_ready, 1)
            for k in range(KD):
                filled(dve, ("x", k))
                freeing(nc.vector.tensor_copy(xT[:, k, LAT], bank(("x", k))))
            for b in range(2):
                filled(dve, ("x", f"ctx{b}"))
                freeing(nc.vector.tensor_copy(xT[:, 4 * b:4 * b + 4, CTX], bank(("x", f"ctx{b}")).rearrange("p (k n) -> p k n", k=4)))
            then(nc.vector.tensor_copy(ident_r[:, :], ident))
            dve.wait_ge(router_hi, 1)
            rest(rt_lo[:, :], arena[:, 12672:12928], rt_hi[:, :]).then_inc(router_lo, 1)
            root_of((0, "norm", 0))
            modulation("start")
            turned_mod(mods.flush())

            for L in range(LAYERS):
                keys = [(kind, sum(k2 == kind for k2, _ in IN[L][:j])) for j, (kind, _) in enumerate(IN[L])]
                if L == 0:
                    for key in keys[:3]:
                        split(key)
                norm(L, 0)
                if L == 0:
                    split(keys[3])
                    split(keys[4])
                    for g in range(4):
                        filled(dve, ("s", g))
                        freeing(nc.vector.tensor_copy(gated[:, g, LAT], bank(("s", g))))
                    filled(dve, ("s", "ctx"))
                    freeing(nc.vector.tensor_copy(gated[:, :, CTX], bank(("s", "ctx")).rearrange("p (m n) -> p m n", m=4)))
                    emptied(dve, ("s", "ctx"))
                    for j in range(2):
                        for m in (2 * j, 2 * j + 1):
                            filled(dve, ("u", m))
                            freeing(nc.vector.tensor_tensor(two(gated[:, m, :]), halves(("u", m)), two(gated[:, m, :]), ALU.mult))
                        split(keys[5 + j])
                    dve.wait_ge(cat_hi, 1)
                    rest(h_lo_[:, 0:4 * T], gated[:, :, :].rearrange("p m n -> p (m n)"), h_hi_[:, 0:4 * T]).then_inc(cat_lo, 1)
                    then(nc.vector.tensor_scalar(stat[:, 6:7], cols[:, R_EVQ:R_EVQ + 1], HD ** -0.5, None, ALU.mult))
                    dve.wait_ge(cs_in, 16)
                    for m in range(5):
                        root_of(("qk norm", m))
                        whole = qT[:, m, :] if m < 4 else kT[:, P:KEYS]
                        gain = stat[:, 6:7] if m < 4 else cols[:, R_EVK:R_EVK + 1]
                        nc.vector.scalar_tensor_tensor(whole, whole, gain, rstd, ALU.mult, ALU.mult).then_inc(proj_norm, 1)
                        modulation(("qk", m))
                        filled(dve, ("qk rot", m))
                        x = whole[:, 0:NL]
                        freeing(nc.vector.tensor_tensor(tmp[0], bank(("qk rot", m)), rope_s, ALU.mult))
                        then(nc.vector.tensor_tensor(x, x, rope_c, ALU.mult))
                        nc.vector.tensor_tensor(x, x, tmp[0], ALU.add).then_inc(roped, 1)
                    turned_mod(mods.flush())
                    filled(dve, "new k")
                    freeing(nc.vector.tensor_copy(small[:, P:2 * P], bank("new k")[:, 0:P]))
                else:
                    for key in keys[3:5]:
                        split(key)
                    emptied(dve, ("gc", 3))
                    for j in range(2):
                        for m in (2 * j, 2 * j + 1):
                            filled(dve, ("hv", m))
                            freeing(nc.vector.tensor_tensor(two(zT[:, m, :]), halves(("hv", m)), two(zT[:, m, :]), ALU.mult))
                        split(keys[5 + j])
                    emptied(dve, ("hv", 3))
                    tap = lambda w, m: cols[:, R_CONV + 4 * w + m:R_CONV + 4 * w + m + 1]
                    for m in range(4):
                        ins = nc.vector.tensor_scalar(yT[:, m, :], zT[:, m, :], tap(1, m), None, ALU.mult)
                    then(ins)
                    for w, lo, zlo in ((0, 1, 0), (2, 0, 1)):
                        for m in range(4):
                            for base, n in ((0, NL), (NL, NC)):
                                y = yT[:, m, base + lo:base + lo + n - 1]
                                ins = nc.vector.scalar_tensor_tensor(y, zT[:, m, base + zlo:base + zlo + n - 1], tap(w, m), y,
                                                                     ALU.mult, ALU.add)
                        then(ins)
                    for m in range(4):
                        filled(dve, ("gb", m))
                        freeing(nc.vector.tensor_tensor(two(yT[:, m, :]), halves(("gb", m)), two(yT[:, m, :]), ALU.mult))
                        if m == 1:
                            split(keys[7])
                    emptied(dve, ("gb", 3))
                    dve.wait_ge(cat_hi, 2)
                    rest(h_lo_[:, 4 * T:8 * T], yT[:, :, :].rearrange("p m n -> p (m n)"), h_hi_[:, 4 * T:8 * T]).then_inc(cat_lo, 1)
                    root_of("cq norm")
                    for m in range(2):
                        ins = nc.vector.scalar_tensor_tensor(cq[:, m, :], cq[:, m, :], cols[:, R_QA + m:R_QA + m + 1], rstd,
                                                             ALU.mult, ALU.mult)
                    ins.then_inc(proj_norm, 1)
                    dve.wait_ge(proj_norm, 6)
                    modulation("cq")
                    root_of("ckv norm")
                    nc.vector.scalar_tensor_tensor(ckv[:, P:KEYS], ckv[:, P:KEYS], cols[:, R_KVA:R_KVA + 1], rstd,
                                                   ALU.mult, ALU.mult).then_inc(proj_norm, 1)
                    modulation("ckv")
                    dve.wait_ge(cs_in, 32)
                    filled(dve, "kr rot")
                    krl = kr[:, P:P + NL]
                    freeing(nc.vector.tensor_tensor(tmp[1][64:96, :], bank("kr rot")[64:96, :], rope_s[64:96, :], ALU.mult))
                    then(nc.vector.tensor_tensor(krl, krl, rope_c[64:96, :], ALU.mult))
                    nc.vector.tensor_tensor(krl, krl, tmp[1][64:96, :], ALU.add).then_inc(roped, 1)
                    modulation("kr")
                    turned_mod(mods.flush())
                    for name, dst, w in (("new ckv", small[:, 160:160 + KVL], KVL), ("new kr", small[:, 288:288 + ROPE], ROPE)):
                        filled(dve, name)
                        freeing(nc.vector.tensor_copy(dst, bank(name)[:, 0:w]))

                def prepare(hh):
                    if L == 0 or hh >= HEADS:
                        return
                    name = ("uq rot", hh)
                    filled(dve, name)
                    x = qh[hh % 2][64:96, LAT]
                    freeing(nc.vector.tensor_tensor(tmp[1][64:96, :], bank(name)[64:96, :], rope_s[64:96, :], ALU.mult))
                    then(nc.vector.tensor_tensor(x, x, rope_c[64:96, :], ALU.mult))
                    nc.vector.tensor_tensor(x, x, tmp[1][64:96, :], ALU.add).then_inc(roped, 1)

                def maximum(i):
                    filled(dve, (L, "S", i))
                    if i >= 2:
                        emptied(dve, (L, "S", i - 2))
                    src = pair((L, "S", i), n=KEYS)
                    ins = nc.vector.tensor_reduce(stat[:, i % 2:i % 2 + 1], src[:, 0:LKEYS], AX.X, ALU.max, negate=True)
                    if STEPS[i][1] == LATE:
                        ins = nc.vector.tensor_reduce(stat[:, 11:12], src[:, LKEYS:KEYS], AX.X, ALU.max, negate=True)
                    ins.then_inc(s_max, 1)

                def normalise(i):
                    emptied(dve, (L, "S", i))
                    late = STEPS[i][1] == LATE
                    r = stat[:, 9 + i % 2:10 + i % 2]
                    ins = nc.vector.reciprocal(r, stat[:, 2 + i % 2:3 + i % 2])
                    if late:
                        ins = nc.vector.reciprocal(stat[:, 13:14], stat[:, 12:13])
                    then(ins)
                    ins = nc.vector.tensor_scalar(prob[i % 2], prob[i % 2], r, None, ALU.mult)
                    if late:
                        ins = nc.vector.tensor_scalar(prob_ctx[L], prob_ctx[L], stat[:, 13:14], None, ALU.mult)
                    ins.then_inc(s_norm, 1)

                def head_out(i):
                    hh, t = STEPS[i]
                    if t < LATE:
                        return
                    r = slice(64 * (hh % 2), 64 * (hh % 2) + 64)
                    kk = (4 if L == 0 else 0) + hh // 2
                    n = 2 * HEADS * L + 2 * hh
                    dve.wait_ge(o_hi, n + 1)
                    freeing(rest(h_lo[r, kk, LAT], bank((L, "O", hh))[r, :], h_hi[r, kk, LAT]))
                    dve.wait_ge(o_hi, n + 2)
                    freeing(rest(h_lo[r, kk, CTX], bank((L, "Oc", hh))[r, 0:NC], h_hi[r, kk, CTX]))

                prepare(0)
                maximum(0)
                for i, (hh, t) in enumerate(STEPS):
                    normalise(i)
                    if i + 1 < len(STEPS):
                        maximum(i + 1)
                    if i >= 1:
                        head_out(i - 1)
                    if PREPARE[t][0] == "uq rot":
                        prepare(hh + PREPARE[t][1])
                    if i in (9, 17, 25):
                        split((L, "out", i // 8 - 1))
                head_out(len(STEPS) - 1)
                for m in range(KD):
                    name = (L, "out", m)
                    filled(dve, name)
                    for src, tk, g in group_halves(name):
                        ins = nc.vector.scalar_tensor_tensor(xT[:, m, tk], src, mod[:, L, 2, m, g:g + 1], xT[:, m, tk], ALU.mult, ALU.add)
                    freeing(ins)
                    if m == 1:
                        split((L, "out", 3))

                norm(L, 1)
                modulation((L, "norm"))
                name = (L, "logits turned")
                filled(dve, name)
                lg = bank(name)[:, 0:NT * E].rearrange("p (t e) -> p t e", t=NT)
                then(nc.vector.tensor_reduce(rowmax, lg, AX.X, ALU.max))
                freeing(nc.vector.tensor_tensor(aff[:, :, :], lg, rowmax.rearrange("p (t o) -> p t o", o=1).to_broadcast([P, NT, E]), ALU.subtract))
                dve.wait_ge(aff_exp, L + 1)
                then(nc.vector.tensor_reduce(rowsum, aff_e[:, :, :], AX.X, ALU.add))
                then(nc.vector.reciprocal(rowsum, rowsum))
                nc.vector.tensor_tensor(aff[:, :, :], aff_e[:, :, :], rowsum.rearrange("p (t o) -> p t o", o=1).to_broadcast([P, NT, E]), ALU.mult)\
                    .then_inc(aff_done, 1)
                modulation((L, "soft"))
                emptied(dve, (L, "aff ctx"))
                for grp, at, cap in ((LAT, 0, CAP_L), (CTX, CAP_L, CAP_C)):
                    for r in range(cap // 8):
                        c8 = slice(at + 8 * r, at + 8 * r + 8)
                        then(nc.vector.max(vals[:, c8], work[:, grp]))
                        then(nc.vector.max_index(idx[:, c8], vals[:, c8], work[:, grp]))
                        then(nc.vector.match_replace(work[:, grp], vals[:, c8], work[:, grp], -1.0))
                then(nc.vector.tensor_copy(idxf, idx))
                nc.vector.tensor_scalar(idxf[:, CAP_L:CAP], idxf[:, CAP_L:CAP], float(NL), None, ALU.add).then_inc(topk_done, 1)
                modulation((L, "top"))
                turned_mod(mods.flush())

                n0 = E * L

                def expert_split(e, what):
                    m0 = piece_number(first(e), what)
                    dve.wait_ge(hi_ready, piece_number(e, what, moe_q[L] + 1))
                    s = PIECE * ((moe_p[L] + m0) % SLOTS)
                    rest(split_slot(w_lo, moe_q[L] + m0), stage[:, s:s + PIECE], split_slot(w_hi, moe_q[L] + m0)).then_inc(lo_ready, 1)

                def rows_split(e):
                    dve.wait_ge(rows_hi, lin(e, 1, n0 + 1))
                    rest(x_lo.rearrange("p (b k) n -> p b (k n)", b=2), psum[:, 0:2, 0:4 * CAP],
                         x_hi.rearrange("p (b k) n -> p b (k n)", b=2)).then_inc(rows_lo, 1)

                def hidden_split(e):
                    dve.wait_ge(hidT_hi, lin(e, 1, n0 + 1))
                    rest(t_lo.rearrange("p f n -> p (f n)"), psum[:, 2, 0:KF * CAP], t_hi.rearrange("p f n -> p (f n)")).then_inc(hidT_lo, 1)

                def hidden(e):
                    dve.wait_ge(silu_done, lin(e, 1, n0 + 1))
                    nc.vector.tensor_tensor(hid, psum[0:CAP, 3, :], sig, ALU.mult).then_inc(hid_ready, 1)

                def step(e, more=True):
                    expert_split(plus(e, 1), "u0")
                    expert_split(plus(e, 1), "u1")
                    hidden_split(e)
                    expert_split(e, "d0")
                    expert_split(e, "d1")
                    if more:
                        rows_split(plus(e, 2))
                        expert_split(plus(e, 2), "g0")
                    hidden(plus(e, 1))
                    if more:
                        expert_split(plus(e, 2), "g1")

                for what in ("g0", "g1", "u0"):
                    expert_split(0, what)
                rows_split(0)
                expert_split(0, "u1")
                expert_split(1, "g0")
                expert_split(1, "g1")
                rows_split(1)
                hidden(0)
                for e in range(3):
                    step(e)
                with dve.Fori(0, (E - 6) // 2) as i:
                    step((i, 3))
                    step((i, 4))
                step(E - 3)
                step(E - 2, False)
                expert_split(E - 1, "d0")
                hidden_split(E - 1)
                expert_split(E - 1, "d1")
                if L + 1 < LAYERS:
                    for key in [(kind, sum(k2 == kind for k2, _ in IN[L + 1][:j])) for j, (kind, _) in enumerate(IN[L + 1])][:3]:
                        split(key)
                add_to_x(L, (L, "moe"), 5)
            norm(LAYERS, 0)


_OUTS = {"y_prompt": (1, NC, D), "y_sample": (1, NL, D), "new_k": (1, 1, KV, NC, HD), "new_v": (1, 1, KV, NC, HD),
         "new_ckv": (1, 1, NC, KVL), "new_kr": (1, 1, NC, ROPE)}


def constants():
    c = np.zeros((P, C_END), np.float32)
    p = np.arange(P)
    c[p, C_ID + p] = 1.0
    c[:, C_ONED:C_ONED + P] = 1.0 / D
    c[:, C_BLK:C_BLK + P] = (p[:, None] // HD == p[None, :] // HD) / HD
    c[:, C_ONE2:C_ONE2 + P] = 1.0 / QL
    c[:, C_ONE1:C_ONE1 + P] = 1.0 / KVL
    for m in range(P):
        low = m % 32 < 16
        c[m + 16 if low else m - 16, C_PERM + m] = -1.0 if low else 1.0
    for m in range(ROPE):
        low = m % 16 < 8
        c[64 + (m + 8 if low else m - 8), C_PERMO + m] = -1.0 if low else 1.0
    sel = np.repeat(np.eye(8, dtype=np.float32), HD, axis=1)

    def table(rot, rows):
        axis = rot // 2
        inv = np.float32(10000.0) ** (-np.arange(0, axis, 2, dtype=np.float32) / np.float32(axis))
        t = np.arange(NL)
        pos = np.stack([t // GRID_W, t % GRID_W]).astype(np.float32)
        d = np.arange(rows) % rot
        ang = pos[d // axis] * inv[d % axis % (axis // 2)][:, None]
        return np.concatenate([np.cos(ang), np.sin(ang)], 1).astype(np.float32)

    return {"const": c, "rope_even": table(HD, P), "rope_odd": table(ROPE, ROPE), "sel": sel}


def kernel(**inputs):
    import concourse.bacc as _bacc
    from concourse.bass_utils import run_bass_kernel_spmd as _run

    nc = _bacc.Bacc("TRN2", target_bir_lowering=False, num_devices=1)
    arrays, args, outs = {}, {}, {}
    for name, value in {**inputs, **constants()}.items():
        v = np.ascontiguousarray(value)
        arrays[f"in_{name}"] = v
        args[name] = nc.dram_tensor(f"in_{name}", v.shape, mybir.dt.from_np(v.dtype), kind="ExternalInput").ap()
    for name, shape in _OUTS.items():
        outs[name] = nc.dram_tensor(f"out_{name}", shape, F32, kind="ExternalOutput").ap()
    trunk(nc, args, outs)
    r = _run(nc, [arrays], core_ids=[0])
    return tuple(r.results[0][f"out_{n}"] for n in _OUTS)
```
